# Optimizing a Trainium2 kernel written in Bass

```python
import math
import jax, jax.numpy as jnp
from jax import lax
import numpy as np

D_MODEL = 1024
BATCH = 1
SEQ = 512
DEPTH = 2

CHUNK = 64
Q_BLOCK = 128
N_MIXERS = 2
HEAD_DIM = 128
N_MEM = 256
MEM_HEADS = 4
MEM_WIDTH = MEM_HEADS * HEAD_DIM
MIX_WIDTH = 2 * D_MODEL
CONV_WIDTH = MIX_WIDTH - MEM_WIDTH
CONV_KERNEL = 31
ATT_HEADS = (MIX_WIDTH - MEM_WIDTH) // HEAD_DIM
ATT_WIDTH = ATT_HEADS * HEAD_DIM
IDX_HEADS = 8
IDX_DIM = 64
TOPK_MAX = 256
ALPHA = (2 * DEPTH) ** 0.25
BETA = (8 * DEPTH) ** -0.25
LN_EPS = 1e-5
NEG = -1e30

A_SIZES = (2 * CONV_WIDTH, MEM_WIDTH, MIX_WIDTH)
B_SIZES = (ATT_WIDTH, HEAD_DIM, HEAD_DIM, IDX_HEADS * IDX_DIM, IDX_DIM, IDX_HEADS, MEM_WIDTH, MIX_WIDTH)
A_IN = sum(A_SIZES)
B_IN = sum(B_SIZES)


def split_cols(h, sizes):
    return jnp.split(h, [int(c) for c in np.cumsum(sizes)[:-1]], axis=-1)

def layer_norm(x, g, b):
    xf = x.astype(jnp.float32)
    mu = xf.mean(-1, keepdims=True)
    var = jnp.square(xf - mu).mean(-1, keepdims=True)
    return ((xf - mu) * lax.rsqrt(var + LN_EPS) * g.astype(jnp.float32) + b.astype(jnp.float32)).astype(x.dtype)

def alibi_slopes(n):
    p = 2 ** int(math.floor(math.log2(n)))
    base = [2.0 ** (-8.0 * (i + 1) / p) for i in range(p)]
    extra = [2.0 ** (-4.0 * (2 * i + 1) / p) for i in range(n - p)]
    return jnp.asarray(base + extra, dtype=jnp.float32)

def mem_cross_attention(q, mem_n, w_mkv):
    B, T, _ = q.shape
    k, v = jnp.split(mem_n @ w_mkv, 2, axis=-1)
    q = q.reshape(B, T, MEM_HEADS, HEAD_DIM)
    k = k.reshape(B, -1, MEM_HEADS, HEAD_DIM)
    v = v.reshape(B, -1, MEM_HEADS, HEAD_DIM)
    s = jnp.einsum('bthd,bnhd->bhtn', q, k).astype(jnp.float32) * (HEAD_DIM ** -0.5)
    p = jax.nn.softmax(s, axis=-1).astype(v.dtype)
    return jnp.einsum('bhtn,bnhd->bthd', p, v).reshape(B, T, MEM_WIDTH)

def conformer_conv(u, conv_w, conv_b, g, b):
    a, gl = jnp.split(u, 2, axis=-1)
    h = a * jax.nn.sigmoid(gl)
    h = jnp.pad(h, ((0, 0), (CONV_KERNEL - 1, 0), (0, 0)))
    h = lax.conv_general_dilated(h, conv_w[:, None, :].astype(h.dtype), (1,), 'VALID',
                                 dimension_numbers=('NWC', 'WIO', 'NWC'),
                                 feature_group_count=CONV_WIDTH) + conv_b
    return jax.nn.silu(layer_norm(h, g, b))

def dsa_attention(q, k, v, q_idx, k_idx, w_idx):
    B, T = q.shape[:2]
    topk = min(TOPK_MAX, T // 4)
    nb = T // Q_BLOCK
    slopes = alibi_slopes(ATT_HEADS)
    key_chunk = jnp.arange(T, dtype=jnp.int32) // CHUNK
    scale = HEAD_DIM ** -0.5

    def to_blocks(a):
        return jnp.moveaxis(a.reshape(B, nb, Q_BLOCK, *a.shape[2:]), 1, 0)

    def block(args):
        qb, qib, wb, start = args
        qpos = start + jnp.arange(Q_BLOCK, dtype=jnp.int32)
        qchunk = qpos // CHUNK
        admiss = key_chunk[None, :] <= qchunk[:, None]
        iscore = jax.nn.relu(jnp.einsum('bqhd,bsd->bqhs', qib, k_idx).astype(jnp.float32))
        iscore = jnp.einsum('bqh,bqhs->bqs', wb.astype(jnp.float32), iscore)
        iscore = jnp.where(admiss[None], iscore, NEG)
        _, sel = lax.top_k(iscore, topk)
        valid = key_chunk[sel] <= qchunk[None, :, None]
        kg = jax.vmap(lambda kb, ib: kb[ib])(k, sel)
        vg = jax.vmap(lambda vb, ib: vb[ib])(v, sel)
        dist = jnp.abs(qpos[None, :, None] - sel).astype(jnp.float32)
        logits = jnp.einsum('bqhd,bqkd->bqhk', qb, kg).astype(jnp.float32) * scale
        logits = logits - slopes[None, None, :, None] * dist[:, :, None, :]
        logits = jnp.where(valid[:, :, None, :], logits, NEG)
        p = jax.nn.softmax(logits, axis=-1).astype(vg.dtype)
        return jnp.einsum('bqhk,bqkd->bqhd', p, vg)

    starts = jnp.arange(nb, dtype=jnp.int32) * Q_BLOCK
    out = lax.map(block, (to_blocks(q), to_blocks(q_idx), to_blocks(w_idx), starts))
    return jnp.moveaxis(out, 0, 1).reshape(B, T, ATT_WIDTH)

def first_inputs(seed: int = 0) -> dict:
    key = jax.random.key(seed)
    ks = jax.random.split(key, 24)
    n_a = (DEPTH + 1) // 2
    n_b = DEPTH // 2
    nrm = lambda k, shape, s: jax.random.normal(k, shape, jnp.float32) * s
    return {
        "x": nrm(ks[0], (BATCH, SEQ, D_MODEL), 1.0),
        "mem": nrm(ks[1], (BATCH, N_MEM, D_MODEL), 1.0),
        "mem_ln_g": 1.0 + nrm(ks[2], (D_MODEL,), 0.05),
        "mem_ln_b": nrm(ks[3], (D_MODEL,), 0.01),
        "a_w_in": nrm(ks[4], (n_a, D_MODEL, A_IN), D_MODEL ** -0.5),
        "a_conv_w": nrm(ks[5], (n_a, CONV_KERNEL, CONV_WIDTH), CONV_KERNEL ** -0.5),
        "a_conv_b": nrm(ks[6], (n_a, CONV_WIDTH), 0.01),
        "a_ln_g": 1.0 + nrm(ks[7], (n_a, CONV_WIDTH), 0.05),
        "a_ln_b": nrm(ks[8], (n_a, CONV_WIDTH), 0.01),
        "a_w_mkv": nrm(ks[9], (n_a, D_MODEL, 2 * MEM_WIDTH), D_MODEL ** -0.5),
        "a_w_out": nrm(ks[10], (n_a, MIX_WIDTH, D_MODEL), BETA * MIX_WIDTH ** -0.5),
        "a_post_g": 1.0 + nrm(ks[11], (n_a, D_MODEL), 0.05),
        "a_post_b": nrm(ks[12], (n_a, D_MODEL), 0.01),
        "b_w_in": nrm(ks[13], (n_b, D_MODEL, B_IN), D_MODEL ** -0.5),
        "b_w_mkv": nrm(ks[14], (n_b, D_MODEL, 2 * MEM_WIDTH), D_MODEL ** -0.5),
        "b_w_out": nrm(ks[15], (n_b, MIX_WIDTH, D_MODEL), BETA * MIX_WIDTH ** -0.5),
        "b_post_g": 1.0 + nrm(ks[16], (n_b, D_MODEL), 0.05),
        "b_post_b": nrm(ks[17], (n_b, D_MODEL), 0.01),
    }

def first_block(x, mem, mem_ln_g, mem_ln_b, a_w_in, a_conv_w, a_conv_b, a_ln_g, a_ln_b,
              a_w_mkv, a_w_out, a_post_g, a_post_b, b_w_in, b_w_mkv, b_w_out,
              b_post_g, b_post_b):
    B, T, _ = x.shape
    mem_n = layer_norm(mem, mem_ln_g, mem_ln_b)
    for i in range(DEPTH):
        j = i // N_MIXERS
        if i % N_MIXERS == 0:
            u, qm, gate = split_cols(x @ a_w_in[j], A_SIZES)
            y_mix = conformer_conv(u, a_conv_w[j], a_conv_b[j], a_ln_g[j], a_ln_b[j])
            w_mkv, w_out, pg, pb = a_w_mkv[j], a_w_out[j], a_post_g[j], a_post_b[j]
        else:
            q, k, v, qi, ki, wi, qm, gate = split_cols(x @ b_w_in[j], B_SIZES)
            y_mix = dsa_attention(q.reshape(B, T, ATT_HEADS, HEAD_DIM), k, v,
                                  qi.reshape(B, T, IDX_HEADS, IDX_DIM), ki, wi)
            w_mkv, w_out, pg, pb = b_w_mkv[j], b_w_out[j], b_post_g[j], b_post_b[j]
        y_mem = mem_cross_attention(qm, mem_n, w_mkv)
        y = jnp.concatenate([y_mix, y_mem], axis=-1) * jax.nn.silu(gate)
        x = layer_norm(ALPHA * x + y @ w_out, pg, pb)
    return x


DEPTH_2 = 1

GRID_W = 64
ATT_HEADS_2 = 8
ATT_KV_HEADS = 2
ATT_HEAD_DIM = 64
ATT_WIDTH_2 = ATT_HEADS_2 * ATT_HEAD_DIM
ATT_KV_WIDTH = ATT_KV_HEADS * ATT_HEAD_DIM
ROPE_THETA = 10000.0
HG_HEADS = 4
HG_DK = 128
HG_DV = 128
HG_WIDTH_K = HG_HEADS * HG_DK
HG_WIDTH_V = HG_HEADS * HG_DV
HG_CHUNK = 64
N_BRANCH = 2
IN_SPLITS = (ATT_WIDTH_2, ATT_KV_WIDTH, ATT_KV_WIDTH,
             HG_WIDTH_K, HG_WIDTH_K, HG_WIDTH_K, HG_WIDTH_V, HG_WIDTH_V,
             N_BRANCH * D_MODEL)
IN_WIDTH = sum(IN_SPLITS)
PEER_HEADS = 8
PEER_NKEYS = 128
PEER_N_EXPERTS = PEER_NKEYS * PEER_NKEYS
PEER_DKEY = 256
PEER_TOPK = 16
PEER_TOKEN_BLOCK = 128
PLE_DIM = 256
EPS = 1e-6


def rmsnorm(x, g):
    xf = x.astype(jnp.float32)
    y = xf * lax.rsqrt(jnp.mean(xf * xf, axis=-1, keepdims=True) + EPS)
    return (y * g.astype(jnp.float32)).astype(x.dtype)

def axial_rope_tables(seq_len):
    rows = seq_len // GRID_W
    row = jnp.repeat(jnp.arange(rows), GRID_W).astype(jnp.float32)
    col = jnp.tile(jnp.arange(GRID_W), rows).astype(jnp.float32)
    axis_dim = ATT_HEAD_DIM // 2
    rot_half = axis_dim // 2
    inv = ROPE_THETA ** (-jnp.arange(rot_half, dtype=jnp.float32) / rot_half)
    ang = jnp.stack([row[:, None] * inv, col[:, None] * inv], axis=1)
    return jnp.cos(ang), jnp.sin(ang)

def apply_axial_rope(x, cos, sin):
    B, S, H, hd = x.shape
    xr = x.reshape(B, S, H, 2, 2, hd // 4).astype(jnp.float32)
    x1, x2 = xr[..., 0, :], xr[..., 1, :]
    c = cos[None, :, None]
    s = sin[None, :, None]
    out = jnp.stack([x1 * c - x2 * s, x1 * s + x2 * c], axis=-2)
    return out.reshape(B, S, H, hd).astype(x.dtype)

def gqa_attention(q, k, v):
    B, S = q.shape[:2]
    G = ATT_HEADS_2 // ATT_KV_HEADS
    nb = S // Q_BLOCK
    scale = ATT_HEAD_DIM ** -0.5
    qb = q.reshape(B, nb, Q_BLOCK, ATT_KV_HEADS, G, ATT_HEAD_DIM).transpose(1, 0, 2, 3, 4, 5)

    def one_block(qblk):
        s = jnp.einsum('bqkgd,bskd->bkgqs', qblk, k, preferred_element_type=jnp.float32) * scale
        pr = jax.nn.softmax(s, axis=-1)
        return jnp.einsum('bkgqs,bskd->bqkgd', pr.astype(v.dtype), v)

    o = lax.map(one_block, qb)
    return o.transpose(1, 0, 2, 3, 4, 5).reshape(B, S, ATT_WIDTH_2)

def gla_chunk_scan(q, k, v, log_f):
    B, S, H, dk = q.shape
    dv = v.shape[-1]
    C = HG_CHUNK
    nc = S // C

    def to_chunks(a):
        return a.reshape(B, nc, C, H, a.shape[-1]).transpose(1, 0, 3, 2, 4)

    qc, kc, vc, gc = to_chunks(q), to_chunks(k), to_chunks(v), to_chunks(log_f)
    lower = jnp.tril(jnp.ones((C, C), dtype=bool))[:, :, None]

    def step(state, inp):
        qi, ki, vi, gi = inp
        b = jnp.cumsum(gi.astype(jnp.float32), axis=2)
        diff = b[:, :, :, None, :] - b[:, :, None, :, :]
        decay = jnp.exp(jnp.where(lower, diff, -jnp.inf))
        A = jnp.einsum('bhtd,bhsd,bhtsd->bhts', qi.astype(jnp.float32), ki.astype(jnp.float32), decay)
        o_intra = jnp.einsum('bhts,bhse->bhte', A, vi.astype(jnp.float32))
        o_inter = jnp.einsum('bhtd,bhde->bhte', qi.astype(jnp.float32) * jnp.exp(b), state)
        b_last = b[:, :, -1:, :]
        k_dec = ki.astype(jnp.float32) * jnp.exp(b_last - b)
        new_state = state * jnp.exp(b_last[:, :, 0, :])[..., None] + \
            jnp.einsum('bhsd,bhse->bhde', k_dec, vi.astype(jnp.float32))
        return new_state, o_intra + o_inter

    state0 = jnp.zeros((B, H, dk, dv), jnp.float32)
    _, o = lax.scan(step, state0, (qc, kc, vc, gc))
    return o.transpose(1, 0, 3, 2, 4).reshape(B, S, H, dv)

def hgrn2_bidirectional(hq, hf_f, hf_b, hi, hg, lb, out_norm):
    B, S = hq.shape[:2]
    q = jax.nn.silu(hq).reshape(B, S, HG_HEADS, HG_DK)
    i_in = hi.reshape(B, S, HG_HEADS, HG_DV)

    def gates(fpre, lbd):
        f = lbd + (1.0 - lbd) * jax.nn.sigmoid(fpre.astype(jnp.float32))
        f = f.reshape(B, S, HG_HEADS, HG_DK)
        return 1.0 - f, jnp.log(f)

    k_f, lf_f = gates(hf_f, lb[0])
    k_b, lf_b = gates(hf_b, lb[1])
    o_fwd = gla_chunk_scan(q, k_f, i_in, lf_f)
    flip = lambda a: jnp.flip(a, axis=1)
    o_bwd = flip(gla_chunk_scan(flip(q), flip(k_b), flip(i_in), flip(lf_b)))
    o = rmsnorm(o_fwd + o_bwd, out_norm)
    o = o * jax.nn.silu(hg.astype(jnp.float32).reshape(B, S, HG_HEADS, HG_DV))
    return o.reshape(B, S, HG_WIDTH_V).astype(hq.dtype)

def peer_ffn(h, w_q, sub_keys, u, v):
    B, S, D = h.shape
    T = B * S
    K = PEER_TOPK
    ht = h.reshape(T, D)
    q = (ht @ w_q).reshape(T, PEER_HEADS, 2, PEER_DKEY // 2)
    s = jnp.einsum('thpc,hpnc->thpn', q, sub_keys, preferred_element_type=jnp.float32)
    v1, i1 = lax.top_k(s[:, :, 0], K)
    v2, i2 = lax.top_k(s[:, :, 1], K)
    cand = (v1[..., :, None] + v2[..., None, :]).reshape(T, PEER_HEADS, K * K)
    cand_idx = (i1[..., :, None] * PEER_NKEYS + i2[..., None, :]).reshape(T, PEER_HEADS, K * K)
    top_s, pos = lax.top_k(cand, K)
    idx = jnp.take_along_axis(cand_idx, pos, axis=-1)
    g = jax.nn.softmax(top_s, axis=-1)
    nb = T // PEER_TOKEN_BLOCK

    def one_block(args):
        xb, ib, gb = args
        ue = jnp.take(u, ib, axis=0)
        a = jnp.einsum('thkd,td->thk', ue, xb, preferred_element_type=jnp.float32)
        w = jax.nn.gelu(a) * gb
        ve = jnp.take(v, ib, axis=0)
        return jnp.einsum('thk,thkd->td', w.astype(ve.dtype), ve)

    out = lax.map(one_block, (ht.reshape(nb, PEER_TOKEN_BLOCK, D),
                              idx.reshape(nb, PEER_TOKEN_BLOCK, PEER_HEADS, K),
                              g.reshape(nb, PEER_TOKEN_BLOCK, PEER_HEADS, K)))
    return out.reshape(B, S, D).astype(h.dtype)

def second_inputs(seed: int = 0) -> dict:
    key = jax.random.key(seed)
    ks = jax.random.split(key, 24)
    f32 = jnp.float32
    nrm = lambda k, shape, scale: jax.random.normal(k, shape, f32) * scale
    gain = lambda k, shape: 1.0 + 0.02 * jax.random.normal(k, shape, f32)
    return {
        "x": nrm(ks[0], (BATCH, SEQ, D_MODEL), 1.0),
        "p": nrm(ks[1], (DEPTH_2, BATCH, SEQ, PLE_DIM), 1.0),
        "norm_mix": gain(ks[2], (DEPTH_2, D_MODEL)),
        "w_in": nrm(ks[3], (DEPTH_2, D_MODEL, IN_WIDTH), D_MODEL ** -0.5),
        "q_norm": gain(ks[4], (DEPTH_2, ATT_HEAD_DIM)),
        "k_norm": gain(ks[5], (DEPTH_2, ATT_HEAD_DIM)),
        "hg_lb_raw": nrm(ks[6], (DEPTH_2 + 1, 2, HG_WIDTH_K), 0.1),
        "hg_out_norm": gain(ks[7], (DEPTH_2, HG_DV)),
        "w_up_att": nrm(ks[8], (DEPTH_2, ATT_WIDTH_2, D_MODEL), ATT_WIDTH_2 ** -0.5),
        "w_up_hg": nrm(ks[9], (DEPTH_2, HG_WIDTH_V, D_MODEL), HG_WIDTH_V ** -0.5),
        "w_out": nrm(ks[10], (DEPTH_2, D_MODEL, D_MODEL), D_MODEL ** -0.5),
        "norm_ffn": gain(ks[11], (DEPTH_2, D_MODEL)),
        "peer_wq": nrm(ks[12], (DEPTH_2, D_MODEL, PEER_HEADS * PEER_DKEY), D_MODEL ** -0.5),
        "peer_subkeys": nrm(ks[13], (DEPTH_2, PEER_HEADS, 2, PEER_NKEYS, PEER_DKEY // 2), (PEER_DKEY // 2) ** -0.5),
        "peer_u": nrm(ks[14], (DEPTH_2, PEER_N_EXPERTS, D_MODEL), D_MODEL ** -0.5),
        "peer_v": nrm(ks[15], (DEPTH_2, PEER_N_EXPERTS, D_MODEL), 0.3),
        "norm_ple": gain(ks[16], (DEPTH_2, D_MODEL)),
        "ple_gate": nrm(ks[17], (DEPTH_2, D_MODEL, D_MODEL), D_MODEL ** -0.5),
        "ple_proj": nrm(ks[18], (DEPTH_2, PLE_DIM, D_MODEL), PLE_DIM ** -0.5),
    }

def second_block(x, p, norm_mix, w_in, q_norm, k_norm, hg_lb_raw, hg_out_norm, w_up_att, w_up_hg,
              w_out, norm_ffn, peer_wq, peer_subkeys, peer_u, peer_v, norm_ple, ple_gate, ple_proj):
    B, S, D = x.shape
    cos, sin = axial_rope_tables(S)
    lb_all = jnp.cumsum(jax.nn.softmax(hg_lb_raw.astype(jnp.float32), axis=0), axis=0)
    offsets = [int(o) for o in np.cumsum(IN_SPLITS)[:-1]]
    for i in range(DEPTH_2):
        h = rmsnorm(x, norm_mix[i])
        proj = h @ w_in[i]
        aq, ak, av, hq, hf_f, hf_b, hi, hg, gate_pre = jnp.split(proj, offsets, axis=-1)
        q = rmsnorm(aq.reshape(B, S, ATT_HEADS_2, ATT_HEAD_DIM), q_norm[i])
        k = rmsnorm(ak.reshape(B, S, ATT_KV_HEADS, ATT_HEAD_DIM), k_norm[i])
        v = av.reshape(B, S, ATT_KV_HEADS, ATT_HEAD_DIM)
        q = apply_axial_rope(q, cos, sin)
        k = apply_axial_rope(k, cos, sin)
        y_att = gqa_attention(q, k, v) @ w_up_att[i]
        y_hg = hgrn2_bidirectional(hq, hf_f, hf_b, hi, hg, lb_all[i], hg_out_norm[i]) @ w_up_hg[i]
        gts = jax.nn.sigmoid(gate_pre.astype(jnp.float32)).reshape(B, S, N_BRANCH, D)
        merged = (gts[:, :, 0] * y_att + gts[:, :, 1] * y_hg).astype(x.dtype)
        x = x + merged @ w_out[i]
        x = x + peer_ffn(rmsnorm(x, norm_ffn[i]), peer_wq[i], peer_subkeys[i], peer_u[i], peer_v[i])
        g_ple = jax.nn.sigmoid(rmsnorm(x, norm_ple[i]) @ ple_gate[i])
        x = x + g_ple * (p[i] @ ple_proj[i])
    return x


def setup_inputs(seed=0):
    out = dict(first_inputs(seed))
    for name, value in second_inputs(seed + 1).items():
        if name != "x":
            out[name + "_2"] = value
    return out


def reference(
    x, mem, mem_ln_g, mem_ln_b, a_w_in, a_conv_w, a_conv_b, a_ln_g, a_ln_b, a_w_mkv, a_w_out,
    a_post_g, a_post_b, b_w_in, b_w_mkv, b_w_out, b_post_g, b_post_b, p_2, norm_mix_2, w_in_2,
    q_norm_2, k_norm_2, hg_lb_raw_2, hg_out_norm_2, w_up_att_2, w_up_hg_2, w_out_2, norm_ffn_2,
    peer_wq_2, peer_subkeys_2, peer_u_2, peer_v_2, norm_ple_2, ple_gate_2, ple_proj_2,
):
    x = first_block(
        x, mem, mem_ln_g, mem_ln_b, a_w_in, a_conv_w, a_conv_b, a_ln_g, a_ln_b, a_w_mkv,
        a_w_out, a_post_g, a_post_b, b_w_in, b_w_mkv, b_w_out, b_post_g, b_post_b,
    )
    return second_block(
        x, p_2, norm_mix_2, w_in_2, q_norm_2, k_norm_2, hg_lb_raw_2, hg_out_norm_2, w_up_att_2,
        w_up_hg_2, w_out_2, norm_ffn_2, peer_wq_2, peer_subkeys_2, peer_u_2, peer_v_2,
        norm_ple_2, ple_gate_2, ple_proj_2,
    )


_drawn_inputs = setup_inputs


def setup_inputs(seed=0):
    import zlib

    import numpy as np

    out = dict(_drawn_inputs(seed))
    spreads = {}
    factors = {'mem_ln_g': 8.0,
     'mem_ln_b': 6.698,
     'a_conv_b': 5.754,
     'a_ln_g': 3.393,
     'a_ln_b': 7.342,
     'b_w_mkv': 3.029,
     'b_post_b': 2.682,
     'norm_mix_2': 3.671,
     'q_norm_2': 8.0,
     'k_norm_2': 8.0,
     'hg_lb_raw_2': 6.561,
     'hg_out_norm_2': 16.009,
     'norm_ffn_2': 22.392,
     'norm_ple_2': 64.0}
    for name, (base, spread) in spreads.items():
        noise = np.random.default_rng([zlib.crc32(name.encode()), seed]).standard_normal(out[name].shape)
        drawn = base * np.exp(spread * noise) if base else spread * noise
        out[name] = __import__('jax').numpy.asarray(drawn.astype(out[name].dtype))
    for name, factor in factors.items():
        out[name] = (out[name] * factor).astype(out[name].dtype)
    return out
```

```python
from contextlib import ExitStack

import numpy as np
import concourse.bass as bass
from concourse import mybir

F32 = mybir.dt.float32
U32 = mybir.dt.uint32
ALU = mybir.AluOpType
ACT = mybir.ActivationFunctionType
AX = mybir.AxisListType
ds = bass.ds

P = 128
T = 512
NB = T // P
D = 1024
KD = D // P
N_MEM = 256
CHUNK = 64
CONV_W = 1536
CONV_T = CONV_W // P
TAPS = 31
HROW = T + TAPS - 1
HEADS_B = 12
IDX_HEADS = 8
TOPK = 128
ALPHA = float(4 ** 0.25)
LN_EPS = 1e-5
RMS_EPS = 1e-6
NEG = -1e30
TAKEN = -3e38
HG_HEADS = 4
LEVELS = 7
ROPE_HEADS = 10
QKV = 768
PEER_HEADS = 8
PEER_K = 16
GROUPS = NB * PEER_HEADS
RING = 4
GELU_C = float(np.sqrt(2 / np.pi))
SCALE128 = float(128 ** -0.5)

SLOTS = {}
POS = {}
UNITS = {}


def _number(table, stages):
    at = 0
    for name, n in stages:
        table[name] = at
        at += n
    table["end"] = at


_number(SLOTS, [("mkv_a", 2), ("mkv_b", 2), ("u", 6), ("gate_a", 4), ("qm_a", 1), ("out_a", 4),
                ("bfm", 4), ("bspec", 1), ("qm_b", 1), ("gate_b", 4), ("out_b", 4),
                ("aq", 1), ("akv", 1), ("hq", 1), ("hff", 1), ("hfb", 1), ("hi", 1), ("hg", 1),
                ("gate_c", 4), ("up", 2), ("out_c", 2), ("wq", 4), ("ple", 2), ("proj", 1)])
_number(POS, [("memT", 8), ("mkv_a", 6), ("mkv_b", 6), ("u", 24), ("gate_a", 16), ("qm_a", 4),
              ("ln", 2), ("out_a", 8), ("xT_a", 8),
              ("bfm", 16), ("bspec", 4), ("vT", 1), ("index", 24), ("qm_b", 4), ("gate_b", 16),
              ("out_b", 8), ("xT_c", 8),
              ("aq", 4), ("akv", 4), ("hq", 4), ("hff", 4), ("hfb", 4), ("hi", 4), ("hg", 4),
              ("gate_c", 16), ("qT", 4), ("kT", 2), ("up", 16), ("mT", 8), ("out_c", 8), ("xT_f", 8),
              ("wq", 16), ("sk", 16), ("xT_p", 8), ("ple", 8), ("proj", 8)])
_number(UNITS, [("mem_a", 2), ("mem_b", 2), ("dsa", 6), ("gqa", 4)])

FM = {}
_number(FM, [("mem_g", 8), ("mem_b", 8), ("conv_b", 12), ("ln_g", 12), ("ln_b", 12),
             ("conv_w", CONV_T * TAPS), ("mix_g", 8), ("ple_g", 8), ("lb0", 8), ("lb1", 8)])
CC = {}
_number(CC, [("ident", P), ("dist", 896), ("adm", P), ("slope", HEADS_B), ("cos", 128), ("sin", 128), ("iota", 16)])


def program(nc, x, xT, mem, wstream, fmvec, rows, norm_rows, consts, levels, subkeys, pT, peer_u, peer_v, out):
    with ExitStack() as ctx:
        def sb(name, shape, dt=F32):
            return ctx.enter_context(nc.sbuf_tensor(name, shape, dt))

        def sem(name):
            return ctx.enter_context(nc.semaphore(name))

        W = sb("W", [P, 2, 4096])
        X = sb("X", [P, NB, D])
        XT = sb("XT", [P, KD, T])
        G = sb("G", [P, 16 * T])
        Y = sb("Y", [P, 16 * T])
        H = sb("H", [P, 18 * T])
        MK = sb("MK", [P, 2, 2048])
        C = sb("C", [P, CC["end"]])
        V = sb("V", [P, FM["end"]])
        SIG = sb("SIG", [P, 4, T])
        ONES = sb("ONES", [P, P])
        QC = sb("QC", [P, 2, T])
        PR = sb("PR", [P, 2, T])
        WI = sb("WI", [P, NB, IDX_HEADS])
        ST = sb("ST", [P, 64])
        MX2 = sb("MX2", [P, 8])
        MX = sb("MX", [P, 4])
        NM = sb("NM", [P, 4])
        SM = sb("SM", [P, 4])
        RI = sb("RI", [P, 4])
        M8 = sb("M8", [P, 8])

        ps = [ctx.enter_context(nc.psum_tensor(f"ps{i}", [P, T], F32)) for i in range(8)]
        SC_BANK, PT_BANK, O_BANK = (ps[4], ps[5]), ps[6], ps[7]

        ident = C[:, 0:P]
        mem_tm = G[:, 0:2 * D]
        memT = Y[:, 0:KD * N_MEM]
        RES = H[:, 0:NB * D]
        L = SIG
        ROW = SIG[:, :, :].rearrange("p (r a) t -> p r (a t)", r=2)
        MU = PR
        PT = H[:, 14 * T:16 * T].rearrange("p (a t) -> p a t", a=2)
        OS = H[:, 16 * T:18 * T].rearrange("p (a t) -> p a t", a=2)
        VT = H[:, 13 * T:14 * T].rearrange("p (b d) -> p b d", b=NB)
        MB = MK[:, 0, 0:3 * T].rearrange("p (b t) -> p b t", b=3)
        TMP = MK[:, 0, 3 * T:4 * T]

        def tm(region, first, width, b, a=0, n=None):
            n = width - a if n is None else n
            return region[:, ds(first * T + b * width + a, n)]

        MKF = MK[:, :, :].rearrange("p a n -> p (a n)")
        XTF = XT[:, :, :].rearrange("p k t -> p (k t)")
        HQ = SIG
        TMPR = H[:, 13 * T:14 * T]
        QKN = QC[:, :, :].rearrange("p a t -> p (a t)")[:, 0:640]
        KK = PR[:, :, :].rearrange("p a (b c) -> p (a b) c", b=2)
        PLE_P = PR
        HROWN = sb("HROWN", [P, P])
        LB = sb("LB", [P, 8])
        OML = sb("OML", [P, 8])
        EB = sb("EB", [P, 4])
        RS = sb("RS", [P, 40])
        ZERO = sb("ZERO", [P, P])
        KF = [H[:, (0 + r) * T:(1 + r) * T] for r in range(2)]
        BF = H[:, 2 * T:3 * T]
        DD = [H[:, (3 + r) * T:(4 + r) * T] for r in range(2)]
        EE = [H[:, (5 + r) * T:(6 + r) * T] for r in range(2)]
        QE = [H[:, (7 + r) * T:(8 + r) * T] for r in range(2)]
        KE = [H[:, (9 + r) * T:(10 + r) * T] for r in range(2)]
        QB = [H[:, (11 + r) * T:(12 + r) * T] for r in range(2)]
        KDEC = H[:, 13 * T:14 * T]
        AS = [H[:, (14 + r) * T:(15 + r) * T] for r in range(2)]
        STATE = [H[:, (16 + r) * T:(17 + r) * T] for r in range(2)]
        KDT = XTF[:, 4 * T:5 * T]
        OH = XTF[:, 5 * T:6 * T]
        OSQ = XTF[:, 6 * T:7 * T]
        LVL = XTF[:, 0:2 * LEVELS * P].rearrange("p (r l t) -> p r l t", r=2, l=LEVELS)
        SUB = MKF[:, 0:2048]
        WS = MKF[:, 2048:2304]
        CAND = H[:, 8 * T:8 * T + 256]
        HOT = XTF[:, 2048:2304]
        small = H[:, 9 * T:10 * T]
        TOPV = small[:, 0:32]
        TOPI = small[:, 32:64].bitcast(U32)
        TOPF = small[:, 64:96]
        BEST = small[:, 96:112]
        BESTI = small[:, 112:128].bitcast(U32)
        PARTI = small[:, 128:160].bitcast(U32)
        PARTF = small[:, 160:192]
        PICK = small[:, 192:224]
        EXPS = small[:, 224:240]
        SUMS = small[:, 240:241]
        RSUM = small[:, 241:242]
        IDX = H[:, 14 * T:15 * T].bitcast(U32)
        GW = H[:, 15 * T:16 * T]
        HC = H[:, 16 * T:18 * T]
        UB = [G[:, k * D:(k + 1) * D] for k in range(RING)]
        VB = [G[:, (RING + k) * D:(RING + k + 1) * D] for k in range(RING)]
        JUNK = [XTF[:, a * D:(a + 1) * D] for a in range(2)]
        DG = [H[:, 12 * T + k * P:12 * T + (k + 1) * P] for k in range(RING)]
        UI = [H[:, 13 * T + a * 16:13 * T + (a + 1) * 16].bitcast(U32) for a in range(2)]
        VI = [H[:, 13 * T + 32 + a * 16:13 * T + 32 + (a + 1) * 16].bitcast(U32) for a in range(2)]
        AA = [H[:, 13 * T + 64 + a * 16:13 * T + 64 + (a + 1) * 16] for a in range(2)]
        WV = [H[:, 13 * T + 96 + a * 16:13 * T + 96 + (a + 1) * 16] for a in range(2)]
        GT = H[:, 13 * T + 128:13 * T + 144]
        TH = H[:, 13 * T + 144:13 * T + 160]
        A_BANK, KV_BANK, HO_BANK = (ps[4], ps[5]), ps[6], ps[7]

        def fm(name, i=0, n=1):
            return V[:, FM[name] + i:FM[name] + i + n]

        def gt(i, n=1):
            return G[:, ds(i * T, n * T)]

        def yt(i, n=1):
            return Y[:, ds(i * T, n * T)]

        def ht(i, n=1):
            return H[:, ds(i * T, n * T)]

        def hrow(i, a, n):
            return H[:, ds(i * HROW + a, n)]

        loaded_x = sem("loaded_x")
        loaded_mem = sem("loaded_mem")
        loaded_const = sem("loaded_const")
        loaded_rows = sem("loaded_rows")
        slot_loaded = [sem("slot_loaded0"), sem("slot_loaded1")]
        slot_used = sem("slot_used")
        bank_full = sem("bank_full")
        bank_free = sem("bank_free")
        passed = {e: sem(f"passed_{e}") for e in ("act", "dve", "pool")}
        dve_link = sem("dve_link")
        act_link = sem("act_link")
        mem_normed = sem("mem_normed")
        glu_free = sem("glu_free")
        glu_done = sem("glu_done")
        conv_tap = sem("conv_tap")
        centred = sem("centred")
        squared = sem("squared")
        squares_used = sem("squares_used")
        scaled = sem("scaled")
        silued = sem("silued")
        mix_gated = sem("mix_gated")
        var_ready = sem("var_ready")
        std_ready = sem("std_ready")
        score_full = sem("score_full")
        score_free = sem("score_free")
        maxed = sem("maxed")
        probs_full = sem("probs_full")
        pT_full = sem("pT_full")
        pT_copied = sem("pT_copied")
        pv_full = sem("pv_full")
        o_free = sem("o_free")
        os_free = sem("os_free")
        q_full = sem("q_full")
        att_gated = sem("att_gated")
        x_normed = sem("x_normed")
        relu_free = sem("relu_free")
        ones_ready = sem("ones_ready")
        loaded_qkn = sem("loaded_qkn")
        loaded_levels = sem("loaded_levels")
        loaded_sub = sem("loaded_sub")
        loaded_p = sem("loaded_p")
        xn_ready = sem("xn_ready")
        qk_part = sem("qk_part")
        rope_done = sem("rope_done")
        kk_ready = sem("kk_ready")
        q_cleared = sem("q_cleared")
        lb_diff = sem("lb_diff")
        lb_sig = sem("lb_sig")
        hg_sig = sem("hg_sig")
        hg_f = sem("hg_f")
        hg_lf = sem("hg_lf")
        hg_diff = sem("hg_diff")
        hg_exp = sem("hg_exp")
        hg_exp_used = sem("hg_exp_used")
        hg_qe = sem("hg_qe")
        hg_ke = sem("hg_ke")
        hg_a_full = sem("hg_a_full")
        hg_a_free = sem("hg_a_free")
        hg_kdec = sem("hg_kdec")
        hg_kT_full = sem("hg_kT_full")
        hg_kT_copied = sem("hg_kT_copied")
        hg_kv_full = sem("hg_kv_full")
        hg_state = sem("hg_state")
        hg_o_full = sem("hg_o_full")
        hg_o_copied = sem("hg_o_copied")
        hg_ms = sem("hg_ms")
        hg_std = sem("hg_std")
        hg_normed = sem("hg_normed")
        hg_oT_full = sem("hg_oT_full")
        hg_y = sem("hg_y")
        up_gated = sem("up_gated")
        merged = sem("merged")
        h_ready = sem("h_ready")
        picked = sem("picked")
        staged = sem("staged")
        u_loaded = [sem(f"u_loaded{k}") for k in range(RING)]
        v_loaded = [sem(f"v_loaded{k}") for k in range(RING)]
        dots = sem("dots")
        v_done = sem("v_done")
        tanh_in = sem("tanh_in")
        tanh_out = sem("tanh_out")
        weights = sem("weights")
        diag_full = sem("diag_full")
        acc_full = sem("acc_full")
        acc_free = sem("acc_free")
        zero_ready = sem("zero_ready")
        y_ready = sem("y_ready")
        stored = sem("stored")

        def hold(eng, name, semaphore, value):
            eng.wait_ge(semaphore, value)
            eng.sem_inc(passed[name], 1)

        class Chain:

            def __init__(self, eng, name, semaphore):
                self.eng, self.name, self.sem, self.n, self.off = eng, name, semaphore, 0, 0

            def link(self, ins):
                self.n += 1
                ins.then_inc(self.sem, 1)
                if isinstance(self.off, int):
                    self.eng.wait_ge(self.sem, self.n)
                else:
                    hold(self.eng, self.name, self.sem, self.off + self.n)

            def loop(self, times, per, body):
                base = self.n
                with self.eng.Fori(0, times) as i:
                    self.off = i * per
                    body(i)
                    assert self.n - base == per, (self.n - base, per)
                self.n, self.off = base + times * per, 0

        FINAL = (y_ready, 1)
        block = ctx.enter_context(nc.Block())

        @block.sync
        def _(sp):
            sp.dma_start(mem_tm.rearrange("p (b d) -> p b d", b=2),
                         mem.rearrange("(b p) d -> p b d", p=P)).then_inc(loaded_mem, 16)
            sp.dma_start(C[:, :], consts).then_inc(loaded_const, 16)
            sp.dma_start(HROWN[:, :], norm_rows[640:768].partition_broadcast(P)).then_inc(loaded_const, 16)
            sp.dma_start(V[:, :], fmvec).then_inc(loaded_const, 16)
            for s in range(2):
                sp.dma_start(W[:, s, :], wstream[s]).then_inc(slot_loaded[s], 16)
            sp.dma_start(XT[:, :, :], xT.rearrange("(k p) t -> p k t", p=P)).then_inc(loaded_x, 16)
            sp.dma_start(X[:, :, :], x.rearrange("(b p) d -> p b d", p=P)).then_inc(loaded_x, 16)
            n = SLOTS["end"]
            with sp.Fori(1, n // 2) as i:
                for s in range(2):
                    sp.wait_ge(slot_used, i * 2 + s - 1)
                    sp.dma_start(W[:, s, :], wstream[ds(i * 2 + s, 1)].rearrange("a p n -> (a p) n")
                                 ).then_inc(slot_loaded[s], 16)
            if n % 2:
                sp.wait_ge(slot_used, n - 2)
                sp.dma_start(W[:, 0, :], wstream[n - 1]).then_inc(slot_loaded[0], 16)
            sp.wait_ge(FINAL[0], FINAL[1])
            sp.dma_start(out.rearrange("a (b p) d -> p (a b) d", p=P), X[:, :, :]).then_inc(stored, 16)
            sp.wait_ge(stored, 16)

        @block.tensor
        def _(pe):
            def bank(pos):
                pe.wait_ge(bank_free, pos + 1)

            def slot(s0, j, i=None):
                s = s0 + j
                pe.wait_ge(slot_loaded[s % 2], 16 * (s // 2 + 1) + (0 if i is None else i * 16))
                return W[:, s % 2, :]

            def project_fm(w, pos0, j, i_pos, rhs, tiles=4):
                w = w.rearrange("p (k n) -> p k n", k=KD)
                for m in range(tiles):
                    bank(i_pos + (pos0 + 4 * j + m))
                    b = ps[(pos0 + m) % 4]
                    for k in range(KD):
                        mm = pe.matmul(b[:, 0:rhs[k].shape[-1]], w[:, k, m * P:(m + 1) * P], rhs[k],
                                       start=(k == 0), stop=(k == KD - 1))
                    mm.then_inc(bank_full, 1)

            def used():
                pe.drain().then_inc(slot_used, 1)

            def stage_fm(name, i=None, slots=2):
                for j in range(slots):
                    w = slot(SLOTS[name], j, i)
                    project_fm(w, POS[name], j, 0 if i is None else i * 4 * slots,
                               [XT[:, k, :] for k in range(KD)])
                    used()

            def mem_kv(name):
                w = slot(SLOTS[name], 0)
                mt = memT.rearrange("p (k n) -> p k n", k=KD)
                project_fm(w, POS[name], 0, 0, [mt[:, k, :] for k in range(KD)])
                used()
                w = slot(SLOTS[name], 1).rearrange("p (k n) -> p k n", k=KD)
                for b in range(2):
                    pos = POS[name] + 4 + b
                    bank(pos)
                    for k in range(KD):
                        mm = pe.matmul(ps[pos % 4][:, :], mt[:, k, b * P:(b + 1) * P], w[:, k, :],
                                       start=(k == 0), stop=(k == KD - 1))
                    mm.then_inc(bank_full, 1)
                used()

            def transposes(pos, parts):
                bank(pos)
                for n, src in enumerate(parts):
                    mm = pe.transpose(ps[pos % 4][:, n * P:(n + 1) * P], src, ident)
                mm.then_inc(bank_full, 1)

            def attention(name, times, unit0, n_keys, k_of, v_of, dv, joined=False):
                with pe.Fori(0, times) as i:
                    place = 0

                    def score_bank():
                        nonlocal place
                        b = SC_BANK[place % 2]
                        pe.wait_ge(score_free, (unit0 + i) * 10 + place + 1)
                        place += 1
                        return b

                    for t in range(11):
                        if t < 8:
                            e, b = t // 4, t % 4
                            if b == 0:
                                pe.wait_ge(q_full, (unit0 + i) * 2 + e + 1)
                            s = score_bank()
                            n = n_keys(b)
                            pe.matmul(s[:, 0:n], QC[:, e, b * P:(b + 1) * P], k_of(i, e, n),
                                      start=True, stop=True).then_inc(score_full, 1)
                        outs = ([0, 1] if t == 10 else []) if joined else {6: [0], 10: [1]}.get(t, [])
                        for e in outs:
                            s = score_bank()
                            pe.wait_ge(o_free, (unit0 + i) * 8 + 1 + (8 if joined else 4 * e + 4))
                            for b in range(2 if joined else 4):
                                mm = pe.transpose(s[:, b * P:(b + 1) * P], OS[:, e, b * P:(b + 1) * P], ident)
                            mm.then_inc(score_full, 1)
                        if 1 <= t <= 8:
                            u = t - 1
                            n = n_keys(u % 4) // P
                            pe.wait_ge(probs_full, (unit0 + i) * 8 + u + 1)
                            pe.wait_ge(pT_copied, (unit0 + i) * 8 + u + 1)
                            for k in range(n):
                                mm = pe.transpose(PT_BANK[:, k * P:(k + 1) * P],
                                                  PR[:, u % 2, k * P:(k + 1) * P], ident)
                            mm.then_inc(pT_full, 1)
                        if 2 <= t <= 9:
                            u = t - 2
                            n = n_keys(u % 4) // P
                            pe.wait_ge(pT_copied, (unit0 + i) * 8 + u + 2)
                            pe.wait_ge(o_free, (unit0 + i) * 8 + u + 1)
                            for k in range(n):
                                mm = pe.matmul(O_BANK[:, 0:dv],
                                               PT[:, u % 2, k * P:(k + 1) * P], v_of(i, u // 4, k),
                                               start=(k == 0), stop=(k == n - 1))
                            mm.then_inc(pv_full, 1)

            def mem_attention(name, layer):
                kT = MK[:, layer, 0:1024]
                v = MK[:, layer, 1024:2048]
                attention(name, 2, UNITS[name], lambda b: N_MEM,
                          lambda i, e, n: kT[:, ds(i * 512 + e * 256, 256)],
                          lambda i, e, k: v[:, ds(i * 256 + e * 128 + k * 512, 128)], P)

            def out_projection(name):
                with pe.Fori(0, 2) as i:
                    for j in range(2):
                        w = slot(SLOTS[name], j, i).rearrange("p (k n) -> p k n", k=KD)
                        for b in range(NB):
                            pos = POS[name] + b
                            if j == 0:
                                bank(i * 4 + pos)
                            for k in range(KD):
                                mm = pe.matmul(ps[pos % 4][:, :],
                                               Y[:, (j * KD + k) * T + b * P:(j * KD + k) * T + (b + 1) * P],
                                               w[:, k, :], start=(j == 0 and k == 0),
                                               stop=(j == 1 and k == KD - 1))
                            if j == 1:
                                mm.then_inc(bank_full, 1)
                        used()

            def x_transposes(name, done):
                pe.wait_ge(x_normed, done)
                for k in range(KD):
                    transposes(POS[name] + k, [X[:, b, k * P:(k + 1) * P] for b in range(NB)])

            pe.sem_inc(hg_a_full, 1)
            pe.wait_ge(loaded_const, 48)
            pe.wait_ge(mem_normed, 1)
            for k in range(KD):
                transposes(POS["memT"] + k, [mem_tm[:, b * D + k * P:b * D + (k + 1) * P] for b in range(2)])
            pe.wait_ge(bank_free, POS["mkv_a"] + 4)
            mem_kv("mkv_a")
            mem_kv("mkv_b")
            pe.wait_ge(loaded_x, 32)
            with pe.Fori(0, 3) as i:
                stage_fm("u", i)
            with pe.Fori(0, 2) as i:
                stage_fm("gate_a", i)
            stage_fm("qm_a", None, 1)
            mem_attention("mem_a", 0)
            pe.wait_ge(conv_tap, CONV_T * TAPS)
            pe.wait_ge(ones_ready, 1)
            pos = POS["ln"]
            bank(pos)
            for c in range(CONV_T):
                mm = pe.matmul(ps[pos % 4][:, :], ONES[:, :], yt(c), start=(c == 0), stop=(c == CONV_T - 1))
            mm.then_inc(bank_full, 1)
            bank(pos + 1)
            for c in range(CONV_T):
                pe.wait_ge(squared, c + 1)
                mm = pe.matmul(ps[(pos + 1) % 4][:, :], ONES[:, :], SIG[:, c % 4, :],
                               start=(c == 0), stop=(c == CONV_T - 1))
                if c < CONV_T - 1:
                    mm.then_inc(squares_used, 1)
            mm.then_inc(bank_full, 1)
            pe.wait_ge(mix_gated, CONV_T)
            pe.wait_ge(att_gated, 4)
            out_projection("out_a")
            x_transposes("xT_a", NB)
            pe.wait_ge(bank_free, POS["bfm"] + 4)
            with pe.Fori(0, 2) as i:
                stage_fm("bfm", i)
            w = slot(SLOTS["bspec"], 0)
            pos = POS["bspec"]
            w3 = w.rearrange("p (k n) -> p k n", k=KD)
            for m in range(3):
                bank(pos + m)
                for k in range(KD):
                    mm = pe.matmul(ps[(pos + m) % 4][:, :], w3[:, k, m * P:(m + 1) * P], XT[:, k, :],
                                   start=(k == 0), stop=(k == KD - 1))
                mm.then_inc(bank_full, 1)
            bank(pos + 3)
            for b in range(NB):
                for k in range(KD):
                    mm = pe.matmul(ps[(pos + 3) % 4][:, b * IDX_HEADS:(b + 1) * IDX_HEADS],
                                   XT[:, k, b * P:(b + 1) * P], w3[:, k, 3 * P:3 * P + IDX_HEADS],
                                   start=(k == 0), stop=(k == KD - 1))
            mm.then_inc(bank_full, 1)
            used()
            pe.wait_ge(bank_free, POS["bfm"] + 14 + 4)
            transposes(POS["vT"], [H[:, 13 * T + b * P:13 * T + (b + 1) * P] for b in range(NB)])
            pe.wait_ge(bank_free, POS["bspec"] + 4 + 4)
            pos = POS["index"]
            for b in range(1, NB):
                for h in range(IDX_HEADS):
                    r = 64 * (h % 2)
                    bank(pos)
                    pe.matmul(ps[pos % 4][:, 0:(b + 1) * P],
                              H[r:r + 64, (14 + h // 2) * T + b * P:(14 + h // 2) * T + (b + 1) * P],
                              QC[r:r + 64, 1, 0:(b + 1) * P],
                              start=True, stop=True).then_inc(bank_full, 1)
                    pos += 1
            stage_fm("qm_b", None, 1)
            with pe.Fori(0, 2) as i:
                stage_fm("gate_b", i)
            mem_attention("mem_b", 1)
            attention("dsa", 6, UNITS["dsa"], lambda b: (b + 1) * P,
                      lambda i, e, n: H[:, 12 * T:12 * T + n],
                      lambda i, e, k: VT[:, k, :], P)
            pe.wait_ge(att_gated, 4 + 4 + 12)
            out_projection("out_b")
            def normed_transposes(name, src, ready, count):
                pe.wait_ge(ready, count)
                for k in range(KD):
                    transposes(POS[name] + k, [src[:, b * D + k * P:b * D + (k + 1) * P] for b in range(NB)])

            def stage_tm(name, i=None, slots=1, n=T):
                for j in range(slots):
                    w = slot(SLOTS[name], j, i).rearrange("p (k n) -> p k n", k=KD)
                    for b in range(NB):
                        p0 = POS[name] + 4 * j + b
                        bank(p0 if i is None else i * (4 * slots) + p0)
                        for k in range(KD):
                            mm = pe.matmul(ps[p0 % 4][:, 0:n], XT[:, k, b * P:(b + 1) * P], w[:, k, 0:n],
                                           start=(k == 0), stop=(k == KD - 1))
                        mm.then_inc(bank_full, 1)
                    used()

            normed_transposes("xT_c", RES, xn_ready, 1)
            pe.wait_ge(bank_free, POS["aq"] + 4)
            stage_tm("aq")
            stage_tm("akv", n=256)
            stage_fm("hq", None, 1)
            stage_fm("hff", None, 1)
            stage_fm("hfb", None, 1)
            stage_tm("hi")
            stage_tm("hg")
            with pe.Fori(0, 2) as i:
                stage_tm("gate_c", i, 2)
            pe.wait_ge(rope_done, NB)
            for m in range(4):
                transposes(POS["qT"] + m, [H[:, 6 * T + b * 640 + m * P:6 * T + b * 640 + (m + 1) * P]
                                           for b in range(NB)])
            pe.wait_ge(kk_ready, 2)
            for g in range(2):
                transposes(POS["kT"] + g, [KK[:, b, g * P:(g + 1) * P] for b in range(NB)])
            pe.wait_ge(bank_free, POS["kT"] + 2 + 4)
            attention("gqa", 4, UNITS["gqa"], lambda b: T,
                      lambda i, e, n: H[:, ds(11 * T + (i // 2) * T, T)],
                      lambda i, e, k: tm(H, 0, QKV, k, 640 + (i // 2) * 64, 64), 64, joined=True)

            pe.wait_ge(loaded_levels, 16)
            with pe.Fori(0, HG_HEADS) as i:
                for r in range(2):
                    unit = i * 2 + r
                    for l in range(LEVELS + 1):
                        pe.wait_ge(hg_a_free, unit * 8 + l + 1)
                        if l < LEVELS:
                            pe.wait_ge(hg_ke, unit * LEVELS + l + 2)
                            pe.wait_ge(hg_qe, unit * LEVELS + l + 1)
                            ke = KE[l % 2]
                        else:
                            ke = KF[r]
                        for c in range(NB):
                            rhs = (QE[l % 2][:, c * P:(c + 1) * P] if l < LEVELS else
                                   HQ[:, :, :].rearrange("p h t -> p (h t)")[:, ds(i * T + c * P, P)])
                            mm = pe.matmul(A_BANK[l % 2][:, c * P:(c + 1) * P], ke[:, c * P:(c + 1) * P], rhs,
                                           start=True, stop=True)
                        mm.then_inc(hg_a_full, 1)
                    pe.wait_ge(hg_kdec, unit + 1)
                    pe.wait_ge(hg_state, unit + 1)
                    for c in range(NB):
                        mm = pe.transpose(KV_BANK[:, c * P:(c + 1) * P], KDEC[:, c * P:(c + 1) * P], ident)
                    mm.then_inc(hg_kT_full, 1)
                    pe.wait_ge(hg_kT_copied, unit + 1)
                    for c in (range(3) if r == 0 else range(1, 4)):
                        mm = pe.matmul(KV_BANK[:, c * P:(c + 1) * P], KDT[:, c * P:(c + 1) * P],
                                       tm(Y, 8, T, c, i * P, P), start=True, stop=True)
                    mm.then_inc(hg_kv_full, 1)
                pe.wait_ge(hg_state, i * 2 + 3)
                pe.wait_ge(hg_y, i + 1)
                pe.wait_ge(hg_a_free, i * 16 + 16 + 2)
                for c in range(NB):
                    v = tm(Y, 8, T, c, i * P, P)
                    parts = [(AS[0][:, c * P:(c + 1) * P], v), (AS[1][:, c * P:(c + 1) * P], v)]
                    if c > 0:
                        parts.append((QB[0][:, c * P:(c + 1) * P], STATE[0][:, c * P:(c + 1) * P]))
                    if c < NB - 1:
                        parts.append((QB[1][:, c * P:(c + 1) * P], STATE[1][:, c * P:(c + 1) * P]))
                    for n, (a, b) in enumerate(parts):
                        mm = pe.matmul(HO_BANK[:, c * P:(c + 1) * P], a, b, start=(n == 0),
                                       stop=(n == len(parts) - 1))
                mm.then_inc(hg_o_full, 1)
                pe.wait_ge(hg_normed, i * NB + NB)
                for c in range(NB):
                    mm = pe.transpose(HO_BANK[:, c * P:(c + 1) * P], OH[:, c * P:(c + 1) * P], ident)
                mm.then_inc(hg_oT_full, 1)
            pe.wait_ge(hg_y, HG_HEADS + 1)
            for j in range(2):
                w = slot(SLOTS["up"], j).rearrange("p (k n) -> p k n", k=4)
                for b in range(NB):
                    for n in range(2):
                        pos = POS["up"] + 8 * j + 2 * b + n
                        bank(pos)
                        for k in range(4):
                            c0 = (4 * j + k) * T + b * P
                            mm = pe.matmul(ps[pos % 4][:, :], Y[:, c0:c0 + P], w[:, k, n * T:(n + 1) * T],
                                           start=(k == 0), stop=(k == 3))
                        mm.then_inc(bank_full, 1)
                used()
            normed_transposes("mT", MKF, up_gated, 1)
            pe.wait_ge(bank_free, POS["out_c"] + 4)
            stage_tm("out_c", None, 2)
            normed_transposes("xT_f", RES, h_ready, 1)
            pe.wait_ge(bank_free, POS["wq"] + 4)
            with pe.Fori(0, 2) as i:
                stage_fm("wq", i)
            pe.wait_ge(loaded_sub, 16)
            pe.wait_ge(bank_free, POS["sk"] + 4)
            for b in range(NB):
                for q in range(4):
                    pos = POS["sk"] + 4 * b + q
                    bank(pos)
                    for n in range(4):
                        hp = 4 * q + n
                        mm = pe.matmul(ps[pos % 4][:, n * P:(n + 1) * P], G[:, hp * T + b * P:hp * T + (b + 1) * P],
                                       SUB[:, hp * P:(hp + 1) * P], start=True, stop=True)
                    mm.then_inc(bank_full, 1)
            pe.wait_ge(zero_ready, 1)
            pe.wait_ge(bank_free, POS["sk"] + 16 + 4)
            pe.sem_inc(v_done, 17)
            with pe.Fori(0, NB) as b:
                pe.wait_ge(acc_free, b + 1)
                for n in range(2):
                    pe.matmul(ps[n][:, :], ZERO[:, :], C[:, 0:T], start=True, stop=False, skip_group_check=True)
                with pe.Fori(0, PEER_HEADS // 2) as j:
                    for s in range(2):
                        g = b * PEER_HEADS + j * 2 + s
                        for k in range(PEER_K):
                            pe.wait_ge(v_loaded[k % RING], g * 64 + 16 * (k // RING + 1))
                            pe.wait_ge(diag_full, g * 16 + k + 1)
                            for n in range(2):
                                mm = pe.matmul(ps[n][:, :], DG[k % RING], VB[k % RING][:, n * T:(n + 1) * T],
                                               start=False, stop=False, skip_group_check=True)
                            mm.then_inc(v_done, 1)
                for n in range(2):
                    mm = pe.matmul(ps[n][:, :], ZERO[:, :], C[:, 0:T], start=False, stop=True,
                                   skip_group_check=True)
                mm.then_inc(acc_full, 1)
            normed_transposes("xT_p", RES, xn_ready, 2)
            pe.wait_ge(bank_free, POS["ple"] + 4)
            stage_tm("ple", None, 2)
            pe.wait_ge(loaded_p, 16)
            w = slot(SLOTS["proj"], 0).rearrange("p (k n) -> p k n", k=4)
            for b in range(NB):
                for n in range(2):
                    pos = POS["proj"] + 2 * b + n
                    bank(pos)
                    for k in range(2):
                        mm = pe.matmul(ps[pos % 4][:, :], PLE_P[:, k, b * P:(b + 1) * P], w[:, k, n * T:(n + 1) * T],
                                       start=(k == 0), stop=(k == 1))
                    mm.then_inc(bank_full, 1)
            used()

        @block.scalar
        def _(act):
            act.sem_inc(bank_free, 4)
            act.sem_inc(score_free, 2)
            act.sem_inc(os_free, 2)
            act.sem_inc(pT_copied, 1)
            act.sem_inc(hg_y, 1)
            ac = Chain(act, "act", act_link)

            def drain(pos, emit, i=None, per=0):
                if i is None:
                    act.wait_ge(bank_full, pos + 1)
                else:
                    hold(act, "act", bank_full, i * per + pos + 1)
                emit(ps[pos % 4]).then_inc(bank_free, 1)

            def copy_to(dst, n=T):
                return lambda b: act.activation(dst, b[:, 0:n], ACT.Copy)

            def mem_kv(name, layer):
                for m in range(4):
                    drain(POS[name] + m, copy_to(MK[:, layer, m * 256:(m + 1) * 256], 256))
                for b in range(2):
                    drain(POS[name] + 4 + b, copy_to(MK[:, layer, 1024 + b * T:1024 + (b + 1) * T]))

            def attention(name, times, biased, n_keys, scale, dst, joined=False):
                unit0 = UNITS[name]
                with act.Fori(0, times) as i:
                    place = 0

                    def scores():
                        nonlocal place
                        hold(act, "act", score_full, (unit0 + i) * 10 + place + 1)
                        place += 1
                        return SC_BANK[(place - 1) % 2]

                    for t in range(11):
                        if t < 8:
                            n = n_keys(t % 4)
                            s = scores()
                            hold(act, "act", maxed, (unit0 + i) * 8 + t + 1)
                            src = L[:, t % 4, 0:n] if biased else s[:, 0:n]
                            act.activation(PR[:, t % 2, 0:n], src, ACT.Exp, bias=NM[:, t % 4:t % 4 + 1],
                                           scale=1.0 if biased else scale,
                                           accum_out=SM[:, t % 4:t % 4 + 1]).then_inc(probs_full, 1)
                            act.sem_inc(passed["act"], 1)
                            hold(act, "act", probs_full, (unit0 + i) * 8 + t + 1)
                            act.sem_inc(score_free, 1)
                        outs = ([0, 1] if t == 10 else []) if joined else {6: [0], 10: [1]}.get(t, [])
                        for e in outs:
                            s = scores()
                            act.activation(dst(i, e), s[:, 0:T // 2 if joined else T], ACT.Copy
                                           ).then_inc(score_free, 1)
                            hold(act, "act", score_free, (unit0 + i) * 10 + place + 2)
                            act.sem_inc(os_free, 1)
                        if 1 <= t <= 8:
                            u = t - 1
                            n = n_keys(u % 4)
                            hold(act, "act", pT_full, (unit0 + i) * 8 + u + 1)
                            act.activation(PT[:, u % 2, 0:n], PT_BANK[:, 0:n], ACT.Copy).then_inc(pT_copied, 1)

            def out_projection(name):
                with act.Fori(0, 2) as i:
                    for b in range(NB):
                        drain(POS[name] + b,
                              lambda bk: act.activation(H[:, ds(i * T + b * D, T)], bk[:, :], ACT.Copy), i, 4)

            def x_transposes(name):
                for k in range(KD):
                    drain(POS[name] + k, copy_to(XT[:, k, :]))

            def load_rows(layer):
                for r in range(2):
                    act.dma_start(ROW[:, r, :], rows[2 * layer + r].partition_broadcast(P)
                                  ).then_inc(loaded_rows, 16)

            act.wait_ge(var_ready, 1)
            act.activation(ST[:, 4:6], ST[:, 4:6], ACT.Sqrt).then_inc(std_ready, 1)
            act.wait_ge(loaded_const, 48)
            for k in range(KD):
                drain(POS["memT"] + k, lambda b: act.activation(
                    memT[:, k * N_MEM:(k + 1) * N_MEM], b[:, 0:N_MEM], ACT.Identity,
                    bias=fm("mem_b", k), scale=fm("mem_g", k)))
            mem_kv("mkv_a", 0)
            mem_kv("mkv_b", 1)
            with act.Fori(0, 3) as i:
                for j in range(4):
                    drain(POS["u"] + j, lambda b: act.activation(hrow(i * 4 + j, TAPS - 1, T), b[:, :], ACT.Copy),
                          i, 8)
                for j in range(4):
                    hold(act, "act", glu_free, i * 4 + j + 1)
                    drain(POS["u"] + 4 + j, lambda b: act.activation(SIG[:, j, :], b[:, :], ACT.Sigmoid), i, 8)
            with act.Fori(0, 2) as i:
                for j in range(8):
                    drain(POS["gate_a"] + j, lambda b: act.activation(gt(i * 8 + j), b[:, :], ACT.Silu), i, 8)
            for j in range(4):
                drain(POS["qm_a"] + j, copy_to(yt(12 + j)))
            attention("mem_a", 2, False, lambda b: N_MEM, SCALE128, lambda i, e: yt(i * 2 + (e + 12)))
            drain(POS["ln"], lambda b: act.activation(MU[:, 0, :], b[:, :], ACT.Copy, scale=1.0 / CONV_W))
            for c in range(CONV_T):
                act.wait_ge(centred, c + 1)
                if c >= 4:
                    act.wait_ge(squares_used, c - 3)
                act.activation(SIG[:, c % 4, :], yt(c), ACT.Square).then_inc(squared, 1)
            drain(POS["ln"] + 1, lambda b: act.activation(MU[:, 1, :], b[:, :], ACT.Copy, scale=1.0 / CONV_W))
            act.wait_ge(var_ready, 2)
            act.activation(MU[:, 1, :], MU[:, 1, :], ACT.Sqrt).then_inc(std_ready, 1)
            load_rows(0)
            for c in range(CONV_T):
                act.wait_ge(scaled, c + 1)
                act.activation(yt(c), yt(c), ACT.Silu, bias=fm("ln_b", c), scale=fm("ln_g", c)
                               ).then_inc(silued, 1)
            out_projection("out_a")
            act.wait_ge(var_ready, 3)
            act.activation(ST[:, 4:8], ST[:, 4:8], ACT.Sqrt).then_inc(std_ready, 1)
            x_transposes("xT_a")
            with act.Fori(0, 2) as i:
                for j in range(8):
                    drain(POS["bfm"] + j, lambda b: act.activation(ht(i * 8 + j), b[:, :], ACT.Copy), i, 8)
            for m in range(2):
                drain(POS["bspec"] + m, copy_to(ht(16 + m)))
            drain(POS["bspec"] + 2, copy_to(QC[:, 1, :]))
            drain(POS["bspec"] + 3, copy_to(WI[:, :, :].rearrange("p b h -> p (b h)"), NB * IDX_HEADS))
            drain(POS["vT"], copy_to(VT[:, :, :].rearrange("p b d -> p (b d)")))
            pos = POS["index"]
            for b in range(1, NB):
                for h in range(IDX_HEADS):
                    act.wait_ge(relu_free, pos - POS["index"] + 1)
                    drain(pos, lambda bk: act.activation(SIG[:, h % 4, 0:(b + 1) * P], bk[:, 0:(b + 1) * P], ACT.Relu))
                    pos += 1
            for j in range(4):
                drain(POS["qm_b"] + j, copy_to(yt(12 + j)))
            with act.Fori(0, 2) as i:
                for j in range(8):
                    drain(POS["gate_b"] + j, lambda b: act.activation(gt(i * 8 + j), b[:, :], ACT.Silu), i, 8)
            attention("mem_b", 2, False, lambda b: N_MEM, SCALE128, lambda i, e: yt(i * 2 + (e + 12)))
            attention("dsa", 6, True, lambda b: (b + 1) * P, SCALE128, lambda i, e: yt(i * 2 + e))
            load_rows(1)
            out_projection("out_b")
            act.wait_ge(var_ready, 4)
            act.activation(ST[:, 4:8], ST[:, 4:8], ACT.Sqrt).then_inc(std_ready, 1)
            act.dma_start(QKN, norm_rows[0:640].partition_broadcast(P)).then_inc(loaded_qkn, 16)
            act.wait_ge(var_ready, 5)
            act.activation(ST[:, 4:8], ST[:, 4:8], ACT.Sqrt).then_inc(std_ready, 1)
            act.wait_ge(lb_diff, 1)
            act.activation(LB[:, :], LB[:, :], ACT.Sigmoid).then_inc(lb_sig, 1)

            def scaled_transposes(name, g):
                for k in range(KD):
                    drain(POS[name] + k, lambda b: act.activation(XT[:, k, :], b[:, :], ACT.Copy, scale=fm(g, k))
                          if g else act.activation(XT[:, k, :], b[:, :], ACT.Copy))

            scaled_transposes("xT_c", "mix_g")
            for b in range(NB):
                drain(POS["aq"] + b, copy_to(tm(H, 0, QKV, b, 0, T)))
            for b in range(NB):
                drain(POS["akv"] + b, copy_to(tm(H, 0, QKV, b, T, 256), 256))
            for m in range(4):
                drain(POS["hq"] + m, lambda b: act.activation(HQ[:, m, :], b[:, :], ACT.Silu))
            for m in range(8):
                drain(POS["hff"] + m, copy_to(MKF[:, m * T:(m + 1) * T]))
            for b in range(NB):
                drain(POS["hi"] + b, copy_to(tm(Y, 8, T, b)))
            for b in range(NB):
                drain(POS["hg"] + b, lambda bk: act.activation(tm(Y, 12, T, b), bk[:, :], ACT.Silu))
            with act.Fori(0, 2) as i:
                for j in range(2):
                    for b in range(NB):
                        drain(POS["gate_c"] + 4 * j + b, lambda bk: act.activation(
                            G[:, ds(b * 2048 + i * D + j * T, T)], bk[:, :], ACT.Sigmoid), i, 8)
            act.dma_start(XTF[:, 0:2 * LEVELS * P], levels).then_inc(loaded_levels, 16)
            act.wait_ge(var_ready, 6)
            act.activation(RS[:, :], RS[:, :], ACT.Sqrt).then_inc(std_ready, 1)
            for m in range(4):
                drain(POS["qT"] + m, copy_to(yt(m)))
            for g in range(2):
                drain(POS["kT"] + g, copy_to(ht(11 + g)))
            attention("gqa", 4, False, lambda b: T, 0.125,
                      lambda i, e: Y[:, ds(i * T + e * (T // 2), T // 2)], joined=True)
            act.dma_start(PLE_P[:, :, :], pT.rearrange("(k p) t -> p k t", p=P)).then_inc(loaded_p, 16)
            with act.Fori(0, HG_HEADS) as i:
                for r in range(2):
                    unit = i * 2 + r
                    hold(act, "act", hg_exp_used, unit * 9 + 1)
                    act.activation(BF, MKF[:, ds(i * T + r * 4 * T, T)], ACT.Sigmoid).then_inc(hg_sig, 1)
                    hold(act, "act", hg_f, unit + 1)
                    act.activation(BF, BF, ACT.Ln).then_inc(hg_lf, 1)
                    for l in range(9):
                        hold(act, "act", hg_exp_used, unit * 9 + max(l - 1, 0) + 1)
                        hold(act, "act", hg_ke, unit * LEVELS + min(max(l - 1, 0), LEVELS) + 1)
                        if l < 8:
                            hold(act, "act", hg_diff, unit * 8 + l + 1)
                        if l < LEVELS:
                            m = 64 >> l
                            d = DD[l % 2].rearrange("p (b h m) -> p b h m", h=2, m=m)
                            e = EE[l % 2].rearrange("p (b h m) -> p b h m", h=2, m=m)
                            act.activation(e[:, :, 0, :], d[:, :, 0, :], ACT.Exp, scale=-1.0 if r == 0 else 1.0)
                            ins = act.activation(e[:, :, 1, :], d[:, :, 1, :], ACT.Exp,
                                                 scale=1.0 if r == 0 else -1.0)
                        elif l == 7:
                            ins = act.activation(EE[1], DD[1], ACT.Exp)
                        else:
                            last = BF.rearrange("p (c t) -> p c t", c=NB)[:, :, P - 1 if r == 0 else 0]
                            act.activation(EB[:, :], last, ACT.Exp)
                            ins = act.activation(EE[0], BF, ACT.Exp)
                        ins.then_inc(hg_exp, 1)
                    hold(act, "act", hg_kT_full, unit + 1)
                    act.activation(KDT, KV_BANK[:, :], ACT.Copy).then_inc(hg_kT_copied, 1)
                hold(act, "act", hg_o_full, i + 1)
                act.activation(OH, HO_BANK[:, :], ACT.Copy).then_inc(hg_o_copied, 1)
                hold(act, "act", hg_ms, i + 1)
                act.activation(RS[:, 0:4], RS[:, 0:4], ACT.Sqrt).then_inc(hg_std, 1)
                hold(act, "act", hg_oT_full, i + 1)
                act.activation(yt(i + 4), HO_BANK[:, :], ACT.Copy).then_inc(hg_y, 1)
            for j in range(2):
                for b in range(NB):
                    for n in range(2):
                        drain(POS["up"] + 8 * j + 2 * b + n,
                              copy_to(tm(MKF if j == 0 else H, 0, D, b, n * T, T)))
            act.wait_ge(up_gated, 1)
            for r in range(1):
                act.dma_start(ROW[:, r, :], rows[4].partition_broadcast(P)).then_inc(loaded_rows, 16)
            scaled_transposes("mT", None)
            act.dma_start(MKF[:, 0:2048], subkeys).then_inc(loaded_sub, 16)
            for j in range(2):
                for b in range(NB):
                    drain(POS["out_c"] + 4 * j + b, copy_to(tm(H, 0, D, b, j * T, T)))
            act.wait_ge(var_ready, 7)
            act.activation(ST[:, 4:8], ST[:, 4:8], ACT.Sqrt).then_inc(std_ready, 1)
            scaled_transposes("xT_f", None)
            with act.Fori(0, 2) as i:
                for j in range(8):
                    drain(POS["wq"] + j, lambda b: act.activation(gt(i * 8 + j), b[:, :], ACT.Copy), i, 8)
            for b in range(NB):
                for q in range(4):
                    drain(POS["sk"] + 4 * b + q, copy_to(Y[:, b * 2048 + q * T:b * 2048 + (q + 1) * T]))
            act.sem_inc(acc_free, 1)
            with act.Fori(0, NB) as b:
                with act.Fori(0, PEER_HEADS // 2) as j:
                    for s in range(2):
                        g = b * PEER_HEADS + j * 2 + s
                        hold(act, "act", tanh_in, g + 1)
                        act.activation(EXPS, GW[:, ds(g * 16, 16)], ACT.Exp, accum_out=SUMS)
                        act.activation(TH, GT, ACT.Tanh, scale=GELU_C).then_inc(tanh_out, 1)
                        hold(act, "act", weights, g + 1)
                        for k in range(PEER_K):
                            hold(act, "act", v_done, g * 16 + k + 14)
                            act.activation(DG[k % RING], ident, ACT.Copy, scale=WV[s][:, k:k + 1]
                                           ).then_inc(diag_full, 1)
                hold(act, "act", acc_full, b + 1)
                act.activation(Y[:, ds(b * D, T)], ps[0][:, :], ACT.Copy)
                act.activation(Y[:, ds(b * D + T, T)], ps[1][:, :], ACT.Copy).then_inc(acc_free, 1)
            act.wait_ge(var_ready, 8)
            act.activation(ST[:, 4:8], ST[:, 4:8], ACT.Sqrt).then_inc(std_ready, 1)
            scaled_transposes("xT_p", "ple_g")
            for j in range(2):
                for b in range(NB):
                    drain(POS["ple"] + 4 * j + b, lambda bk: act.activation(tm(G, 0, D, b, j * T, T), bk[:, :],
                                                                            ACT.Sigmoid))
            for b in range(NB):
                for n in range(2):
                    drain(POS["proj"] + 2 * b + n, copy_to(tm(Y, 0, D, b, n * T, T)))

        @block.gpsimd
        def _(pool):
            pool.sem_inc(glu_free, 4)
            pool.sem_inc(hg_ke, 1)
            with pool.Fori(0, 3) as i:
                for j in range(4):
                    hold(pool, "pool", bank_free, i * 8 + POS["u"] + 4 + j + 1 + 4)
                    pool.tensor_tensor(hrow(i * 4 + j, TAPS - 1, T), hrow(i * 4 + j, TAPS - 1, T),
                                       SIG[:, j, :], ALU.mult).then_inc(glu_done, 1)
                    hold(pool, "pool", glu_done, i * 4 + j + 1)
                    pool.sem_inc(glu_free, 1)

            def stage_q(src, i, e):
                pool.tensor_copy(QC[:, e, :], src(i, e)).then_inc(q_full, 1)

            def gate(dst, i, e, n):
                pool.tensor_tensor(dst(i, e), dst(i, e), gt_of(dst, i, e), ALU.mult).then_inc(att_gated, 1)

            def attention(name, times, q_of, y_first):
                unit0 = UNITS[name]
                for e in range(2):
                    pool.tensor_copy(QC[:, e, :], q_of(0, e)).then_inc(q_full, 1)

                def gate_pair(i):
                    for e in range(2):
                        hold(pool, "pool", score_free, (unit0 + i) * 10 + (8, 10)[e] + 2)
                        pool.tensor_tensor(yt(i * 2 + (e + y_first)), yt(i * 2 + (e + y_first)),
                                           gt(i * 2 + (e + y_first)), ALU.mult).then_inc(att_gated, 1)

                with pool.Fori(0, times - 1) as i:
                    for e in range(2):
                        hold(pool, "pool", score_full, (unit0 + i) * 10 + (4, 9)[e])
                        pool.tensor_copy(QC[:, e, :], q_of(i + 1, e)).then_inc(q_full, 1)
                    gate_pair(i)
                gate_pair(times - 1)

            pool.wait_ge(bank_free, POS["qm_a"] + 4 + 4)
            attention("mem_a", 2, lambda i, e: yt(i * 2 + (e + 12)), 12)
            for c in range(CONV_T):
                pool.wait_ge(silued, c + 1)
                pool.tensor_tensor(yt(c), yt(c), gt(c), ALU.mult).then_inc(mix_gated, 1)
            pool.wait_ge(bank_free, POS["gate_b"] + 16 + 4)
            attention("mem_b", 2, lambda i, e: yt(i * 2 + (e + 12)), 12)
            pool.wait_ge(score_full, UNITS["mem_b"] * 10 + 20)
            attention("dsa", 6, lambda i, e: ht(i * 2 + e), 0)
            pool.wait_ge(rope_done, NB)
            for g in range(2):
                rot = H[:, 6 * T:6 * T + NB * 640].rearrange("p (b c) -> p b c", b=NB)
                for half in range(2):
                    ins = pool.tensor_copy(KK[:, :, g * P + half * 64:g * P + (half + 1) * 64],
                                           rot[:, :, T + g * 64:T + (g + 1) * 64])
                ins.then_inc(kk_ready, 1)
            pool.wait_ge(kk_ready, 2)
            pool.memset(QC[64:P, 0, :], 0.0).then_inc(q_cleared, 1)
            pool.wait_ge(q_cleared, 1)
            pool.memset(QC[0:64, 1, :], 0.0).then_inc(q_cleared, 1)
            pool.wait_ge(q_cleared, 2)
            pool.wait_ge(bank_free, POS["qT"] + 4 + 4)
            for e in range(2):
                pool.tensor_copy(QC[64 * e:64 * e + 64, e, :], Y[64 * e:64 * e + 64, 0:T]).then_inc(q_full, 1)
                pool.wait_ge(q_full, UNITS["gqa"] * 2 + e + 1)
            with pool.Fori(0, 3) as i:
                for e in range(2):
                    hold(pool, "pool", score_full, (UNITS["gqa"] + i) * 10 + (4, 8)[e])
                    pool.tensor_copy(QC[64 * e:64 * e + 64, e, :], Y[64 * e:64 * e + 64, ds(i * T + T, T)]
                                     ).then_inc(q_full, 1)
                    hold(pool, "pool", q_full, (UNITS["gqa"] + i) * 2 + 3 + e)
            with pool.Fori(0, HG_HEADS) as i:
                for r in range(2):
                    unit = i * 2 + r
                    for l in range(LEVELS):
                        hold(pool, "pool", hg_a_full, unit * 8 + max(l - 1, 0) + 1)
                        hold(pool, "pool", hg_exp, unit * 9 + l + 1)
                        pool.tensor_tensor(KE[l % 2], KF[r], EE[l % 2], ALU.mult).then_inc(hg_ke, 1)
            for b in range(NB):
                pool.wait_ge(bank_free, POS["up"] + 2 * b + 2 + 4)
                ins = pool.tensor_tensor(tm(MKF, 0, D, b), tm(MKF, 0, D, b), G[:, b * 2048:b * 2048 + D], ALU.mult)
                ins.then_inc(merged, 1)
            def gather(table, buf, index, loaded, k):
                pool.indirect_dma_start(buf[k % RING], None, table,
                                        bass.IndirectOffsetOnAxis(ap=index[:, k:k + 1], axis=0)
                                        ).then_inc(loaded[k % RING], 16)

            pool.wait_ge(picked, 1)
            pool.tensor_copy(UI[0], IDX[:, 0:16]).then_inc(staged, 1)
            pool.wait_ge(staged, 1)
            for k in range(PEER_K):
                pool.wait_ge(dots, k + 13)
                gather(peer_u, UB, UI[0], u_loaded, k)

            def pair(g, s, last):
                if not last:
                    hold(pool, "pool", picked, g + 2)
                    hold(pool, "pool", dots, g * 16 + 16)
                    pool.tensor_copy(UI[(s + 1) % 2], IDX[:, ds(g * 16 + 16, 16)]).then_inc(staged, 1)
                hold(pool, "pool", v_done, g * 16 + 1)
                pool.tensor_copy(VI[s], IDX[:, ds(g * 16, 16)]).then_inc(staged, 1)
                hold(pool, "pool", staged, g * 2 + (2 if last else 3))
                for k in range(PEER_K):
                    if not last:
                        hold(pool, "pool", dots, g * 16 + 16 + k + 13)
                        gather(peer_u, UB, UI[(s + 1) % 2], u_loaded, k)
                    hold(pool, "pool", v_done, g * 16 + k + 14)
                    gather(peer_v, VB, VI[s], v_loaded, k)

            with pool.Fori(0, GROUPS // 2 - 1) as i:
                for s in range(2):
                    pair(i * 2 + s, s, False)
            pair(GROUPS - 2, 0, False)
            pair(GROUPS - 1, 1, True)

        @block.vector
        def _(dve):
            ch = Chain(dve, "dve", dve_link)
            dve.sem_inc(o_free, 1)
            dve.sem_inc(relu_free, 4)
            dve.sem_inc(hg_exp_used, 1)
            dve.sem_inc(hg_state, 1)

            def row_norm(src, blocks, dst, g, b, done, eps, n):
                for k in range(blocks):
                    for h in range(2):
                        ch.link(dve.bn_stats(ST[:, 8 + 12 * k + 6 * h:14 + 12 * k + 6 * h],
                                             src(k)[:, h * 512:(h + 1) * 512]))
                    ch.link(dve.bn_aggr(MX2[:, 2 * k:2 * k + 2], ST[:, 8 + 12 * k:20 + 12 * k]))
                mv = MX2[:, 0:2 * blocks].rearrange("p (k two) -> p k two", two=2)
                dve.tensor_scalar(ST[:, 4:4 + blocks], mv[:, :, 1], eps, None, ALU.add).then_inc(var_ready, 1)
                dve.wait_ge(std_ready, n)
                ch.link(dve.reciprocal(ST[:, 0:blocks], ST[:, 4:4 + blocks]))
                for k in range(blocks):
                    last = dve.tensor_scalar(dst(k), src(k), mv[:, k, 0:1], ST[:, k:k + 1],
                                             ALU.subtract, ALU.mult)
                    if g is not None:
                        ch.link(last)
                        ch.link(dve.tensor_tensor(dst(k), dst(k), g, ALU.mult))
                        last = dve.tensor_tensor(dst(k), dst(k), b, ALU.add)
                    if k == blocks - 1 or g is not None:
                        last.then_inc(done, 1)
                    else:
                        ch.link(last)

            def attention(name, times, biased, n_keys, scale, dv, joined=False):
                unit0 = UNITS[name]
                places = [0, 1, 2, 3, 4, 5, 6, 7] if joined else [0, 1, 2, 3, 4, 5, 6, 8]
                per = 8 * ((3 if biased else 2) + 1)

                def body(i):
                    for t in range(10):
                        if t < 8:
                            b = t % 4
                            n = n_keys(b)
                            mx, nm = MX[:, b:b + 1], NM[:, b:b + 1]
                            s = SC_BANK[places[t] % 2]
                            if biased:
                                bias = C[:, CC["adm"]:CC["adm"] + P] if b == 0 else MB[:, b - 1, 0:n]
                                d0 = CC["dist"] + 384 - b * P
                                ch.link(dve.scalar_tensor_tensor(
                                    TMP[:, 0:n], C[:, d0:d0 + n], C[:, ds(i * 2 + (CC["slope"] + t // 4), 1)],
                                    bias, ALU.mult, ALU.add))
                                hold(dve, "dve", score_full, (unit0 + i) * 10 + places[t] + 1)
                                ch.link(dve.tensor_tensor_reduce(
                                    out=L[:, b, 0:n], in0=s[:, 0:n], in1=TMP[:, 0:n], scale=scale,
                                    scalar=-3e38, op0=ALU.add, op1=ALU.max, accum_out=mx))
                                dve.tensor_scalar(nm, mx, -1.0, None, ALU.mult).then_inc(maxed, 1)
                                hold(dve, "dve", maxed, (unit0 + i) * 8 + t + 1)
                                ch.link(dve.tensor_scalar(mx, nm, 1.0, None, ALU.mult))
                            else:
                                hold(dve, "dve", score_full, (unit0 + i) * 10 + places[t] + 1)
                                ch.link(dve.tensor_reduce(mx, s[:, 0:n], AX.X, ALU.max))
                                dve.tensor_scalar(nm, mx, -scale, None, ALU.mult).then_inc(maxed, 1)
                                hold(dve, "dve", maxed, (unit0 + i) * 8 + t + 1)
                                ch.link(dve.tensor_scalar(mx, nm, 1.0, None, ALU.mult))
                        if t >= 2:
                            u = t - 2
                            e, b = u // 4, u % 4
                            hold(dve, "dve", pv_full, (unit0 + i) * 8 + u + 1)
                            ch.link(dve.reciprocal(RI[:, b:b + 1], SM[:, b:b + 1]))
                            if joined:
                                if u in (0, 2):
                                    hold(dve, "dve", os_free, (unit0 + i) * 2 + u // 2 + 1)
                                dst = OS[:, b // 2, (b % 2) * P + e * dv:(b % 2) * P + (e + 1) * dv]
                            else:
                                if b == 0:
                                    hold(dve, "dve", os_free, (unit0 + i) * 2 + e + 1)
                                dst = OS[:, e, b * P:(b + 1) * P]
                            dve.tensor_scalar(dst, O_BANK[:, 0:dv], RI[:, b:b + 1], None,
                                              ALU.mult).then_inc(o_free, 1)

                ch.loop(times, per, body)

            dve.memset(ONES[:, :], 1.0).then_inc(ones_ready, 1)
            dve.wait_ge(loaded_mem, 16)
            row_norm(lambda k: mem_tm[:, k * D:(k + 1) * D], 2, lambda k: mem_tm[:, k * D:(k + 1) * D],
                     None, None, mem_normed, LN_EPS, 1)
            hp = H[:, 0:CONV_T * HROW].rearrange("p (c t) -> p c t", c=CONV_T)
            ch.link(dve.memset(hp[:, :, 0:TAPS - 1], 0.0))
            dve.wait_ge(loaded_const, 48)
            with dve.Fori(0, CONV_T // 2) as i:
                for k in range(TAPS):
                    for j in range(2):
                        c = i * 2 + j
                        if k == 0:
                            hold(dve, "dve", glu_done, c + 1)
                            ins = dve.tensor_scalar(yt(c), hrow(c, k, T), V[:, ds(c * TAPS + FM["conv_w"], 1)],
                                                    V[:, ds(c + FM["conv_b"], 1)], ALU.mult, ALU.add)
                        else:
                            dve.wait_ge(conv_tap, i * (2 * TAPS) + (2 * k + j - 1))
                            ins = dve.scalar_tensor_tensor(yt(c), hrow(c, k, T),
                                                           V[:, ds(c * TAPS + (FM["conv_w"] + k), 1)],
                                                           yt(c), ALU.mult, ALU.add)
                        ins.then_inc(conv_tap, 1)
            attention("mem_a", 2, False, lambda b: N_MEM, SCALE128, P)
            dve.wait_ge(bank_free, POS["ln"] + 1 + 4)
            for c in range(CONV_T):
                dve.tensor_tensor(yt(c), yt(c), MU[:, 0, :], ALU.subtract).then_inc(centred, 1)
            dve.wait_ge(bank_free, POS["ln"] + 2 + 4)
            dve.tensor_scalar(MU[:, 1, :], MU[:, 1, :], LN_EPS, None, ALU.add).then_inc(var_ready, 1)
            dve.wait_ge(std_ready, 2)
            ch.link(dve.reciprocal(MU[:, 0, :], MU[:, 1, :]))
            for c in range(CONV_T):
                dve.tensor_tensor(yt(c), yt(c), MU[:, 0, :], ALU.mult).then_inc(scaled, 1)

            def layer_end(name, n, rows_at):
                dve.wait_ge(bank_free, POS[name] + 8 + 4)
                for b in range(NB):
                    ch.link(dve.scalar_tensor_tensor(X[:, b, :], X[:, b, :], ALPHA, RES[:, b * D:(b + 1) * D],
                                                     ALU.mult, ALU.add))
                dve.wait_ge(loaded_rows, 32 * rows_at)
                row_norm(lambda k: X[:, k, :], NB, lambda k: X[:, k, :], ROW[:, 0, :], ROW[:, 1, :],
                         x_normed, LN_EPS, n)

            dve.wait_ge(loaded_x, 32)
            layer_end("out_a", 3, 1)
            dve.wait_ge(x_normed, NB)
            for b in range(1, NB):
                n = (b + 1) * P
                for h in range(IDX_HEADS):
                    dve.wait_ge(bank_free, POS["index"] + (b - 1) * IDX_HEADS + h + 1 + 4)
                    w = WI[:, b, h:h + 1]
                    if h == 0:
                        ins = dve.tensor_scalar(MB[:, b - 1, 0:n], SIG[:, h % 4, 0:n], w, None, ALU.mult)
                    else:
                        ins = dve.scalar_tensor_tensor(MB[:, b - 1, 0:n], SIG[:, h % 4, 0:n], w,
                                                       MB[:, b - 1, 0:n], ALU.mult, ALU.add)
                    ins.then_inc(relu_free, 1)
                    dve.wait_ge(relu_free, 4 + (b - 1) * IDX_HEADS + h + 1)
                adm = C[:, CC["adm"]:CC["adm"] + P]
                ch.link(dve.tensor_tensor(MB[:, b - 1, n - P:n], MB[:, b - 1, n - P:n], adm, ALU.add))

                def take(i):
                    ch.link(dve.max(M8[:, :], MB[:, b - 1, 0:n]))
                    ch.link(dve.match_replace(MB[:, b - 1, 0:n], M8[:, :], MB[:, b - 1, 0:n], TAKEN))

                ch.loop(TOPK // 8, 2, take)
                ch.link(dve.tensor_scalar(MB[:, b - 1, 0:n], MB[:, b - 1, 0:n], -2e38, NEG, ALU.is_ge, ALU.mult))
                ch.link(dve.tensor_tensor(MB[:, b - 1, n - P:n], MB[:, b - 1, n - P:n], adm, ALU.add))
            attention("mem_b", 2, False, lambda b: N_MEM, SCALE128, P)
            attention("dsa", 6, True, lambda b: (b + 1) * P, SCALE128, P)
            layer_end("out_b", 4, 2)
            dve.wait_ge(x_normed, 2 * NB)

            def rms_rows(n):
                for b in range(NB):
                    ch.link(dve.tensor_tensor_reduce(out=RES[:, b * D:(b + 1) * D], in0=X[:, b, :], in1=X[:, b, :],
                                                     scale=1.0, scalar=0.0, op0=ALU.mult, op1=ALU.add,
                                                     accum_out=ST[:, 8 + b:9 + b]))
                dve.tensor_scalar(ST[:, 4:8], ST[:, 8:12], 1.0 / D, RMS_EPS, ALU.mult, ALU.add).then_inc(var_ready, 1)
                dve.wait_ge(std_ready, n)
                ch.link(dve.reciprocal(ST[:, 0:4], ST[:, 4:8]))
                for b in range(NB):
                    ins = dve.tensor_scalar(RES[:, b * D:(b + 1) * D], X[:, b, :], ST[:, b:b + 1], None, ALU.mult)
                    if b < NB - 1:
                        ch.link(ins)
                return ins

            rms_rows(5).then_inc(xn_ready, 1)
            dve.tensor_tensor(LB[:, :], fm("lb0", 0, 8), fm("lb1", 0, 8), ALU.subtract).then_inc(lb_diff, 1)
            dve.wait_ge(lb_sig, 1)
            ch.link(dve.tensor_scalar(OML[:, :], LB[:, :], -1.0, 1.0, ALU.mult, ALU.add))
            dve.wait_ge(bank_free, POS["akv"] + 4 + 4)
            rot = H[:, 6 * T:6 * T + NB * 640].rearrange("p (b c) -> p b c", b=NB)
            for b in range(NB):
                src = tm(H, 0, QKV, b, 0, 640)
                ch.link(dve.tensor_tensor(rot[:, b, :], src, src, ALU.mult))
                ch.link(dve.tensor_reduce(RS[:, 10 * b:10 * b + 10], rot[:, b, :].rearrange("p (h d) -> p h d", d=64),
                                          AX.X, ALU.add))
            dve.tensor_scalar(RS[:, :], RS[:, :], 1.0 / 64, RMS_EPS, ALU.mult, ALU.add).then_inc(var_ready, 1)
            dve.wait_ge(std_ready, 6)
            ch.link(dve.reciprocal(RS[:, :], RS[:, :]))
            dve.wait_ge(loaded_qkn, 16)
            for b in range(NB):
                src = tm(H, 0, QKV, b, 0, 640)
                s3 = src.rearrange("p (h d) -> p h d", d=64)
                scale = RS[:, 10 * b:10 * b + 10].rearrange("p (h o) -> p h o", o=1).broadcast_to([P, ROPE_HEADS, 64])
                ch.link(dve.tensor_tensor(s3, s3, scale, ALU.mult))
                ch.link(dve.tensor_tensor(src, src, QKN, ALU.mult))
                s5 = src.rearrange("p (h a x d) -> p h a x d", h=ROPE_HEADS, a=2, x=2)
                r5 = rot[:, b, :].rearrange("p (h a x d) -> p h a x d", h=ROPE_HEADS, a=2, x=2)
                cos, sin = ([C[:, CC[t] + 32 * b:CC[t] + 32 * b + 32].rearrange("p (o a d) -> p o a d", o=1, a=2)
                             .broadcast_to([P, ROPE_HEADS, 2, 16]) for t in ("cos", "sin")])
                t4 = TMPR[:, 0:320].rearrange("p (h a d) -> p h a d", h=ROPE_HEADS, a=2)
                x1, x2, y1, y2 = s5[:, :, :, 0, :], s5[:, :, :, 1, :], r5[:, :, :, 0, :], r5[:, :, :, 1, :]
                ch.link(dve.tensor_tensor(y1, x1, cos, ALU.mult))
                ch.link(dve.tensor_tensor(t4, x2, sin, ALU.mult))
                ch.link(dve.tensor_tensor(y1, y1, t4, ALU.subtract))
                ch.link(dve.tensor_tensor(y2, x1, sin, ALU.mult))
                ch.link(dve.tensor_tensor(t4, x2, cos, ALU.mult))
                dve.tensor_tensor(y2, y2, t4, ALU.add).then_inc(rope_done, 1)
                dve.wait_ge(rope_done, b + 1)
            attention("gqa", 4, False, lambda b: T, 0.125, 64, joined=True)
            dve.wait_ge(score_free, UNITS["end"] * 10 + 2)
            dve.wait_ge(loaded_levels, 16)
            dve.sem_inc(hg_a_free, 2)
            for r in range(2):
                ch.link(dve.memset(AS[r], 0.0))
            hq = HQ[:, :, :].rearrange("p h t -> p (h t)")

            def recurrence(i):
                for r in range(2):
                    unit = i * 2 + r
                    hold(dve, "dve", hg_sig, unit + 1)
                    at = i + 4 * r
                    ch.link(dve.tensor_scalar(BF, BF, OML[:, ds(at, 1)], LB[:, ds(at, 1)], ALU.mult, ALU.add))
                    dve.tensor_scalar(KF[r], BF, -1.0, 1.0, ALU.mult, ALU.add).then_inc(hg_f, 1)
                    hold(dve, "dve", hg_lf, unit + 1)
                    for c in range(NB):
                        seg = BF[:, c * P:(c + 1) * P]
                        out = DD[1][:, c * P:(c + 1) * P]
                        if r == 1:
                            seg, out = seg[:, ::-1], out[:, ::-1]
                        ins = dve.tensor_tensor_scan(out, ONES[:, :], seg, 0.0, ALU.mult, ALU.add)
                    ch.link(ins)
                    ch.link(dve.tensor_copy(BF, DD[1]))

                    def add_level(l):
                        hold(dve, "dve", hg_a_full, unit * 8 + l + 2)
                        mask = (LVL[:, r, l, :] if l < LEVELS else ident).rearrange("p (o t) -> p o t", o=1)
                        dve.copy_predicated(AS[r].rearrange("p (c t) -> p c t", c=NB),
                                            mask.bitcast(U32).broadcast_to([P, NB, P]),
                                            A_BANK[l % 2][:, :].rearrange("p (c t) -> p c t", c=NB)
                                            ).then_inc(hg_a_free, 1)

                    for t in range(10):
                        if t < 8:
                            if t < LEVELS:
                                m = 64 >> t
                                b3 = BF.rearrange("p (b m) -> p b m", m=2 * m)
                                d3 = DD[t % 2].rearrange("p (b m) -> p b m", m=2 * m)
                                at = m - 1 if r == 0 else m
                                ref = b3[:, :, at:at + 1].broadcast_to([P, T // (2 * m), 2 * m])
                                ins = dve.tensor_tensor(d3, b3, ref, ALU.subtract)
                            else:
                                b3 = BF.rearrange("p (c t) -> p c t", c=NB)
                                d3 = DD[1].rearrange("p (c t) -> p c t", c=NB)
                                at = P - 1 if r == 0 else 0
                                ref = b3[:, :, at:at + 1].broadcast_to([P, NB, P])
                                ins = dve.tensor_tensor(d3, ref, b3, ALU.subtract)
                            ins.then_inc(hg_diff, 1)
                        if 1 <= t:
                            l = t - 1
                            hold(dve, "dve", hg_exp, unit * 9 + l + 1)
                            if l < LEVELS:
                                ins = dve.tensor_tensor(QE[l % 2], hq[:, ds(i * T, T)], EE[l % 2], ALU.mult)
                                ins.then_inc(hg_qe, 1)
                                hold(dve, "dve", hg_qe, unit * LEVELS + l + 1)
                            elif l == 7:
                                dve.tensor_tensor(KDEC, KF[r], EE[1], ALU.mult).then_inc(hg_kdec, 1)
                                hold(dve, "dve", hg_kdec, unit + 1)
                            else:
                                ch.link(dve.tensor_tensor(QB[r], hq[:, ds(i * T, T)], EE[0], ALU.mult))
                            dve.sem_inc(hg_exp_used, 1)
                        if 2 <= t:
                            add_level(t - 2)
                    hold(dve, "dve", hg_kv_full, unit + 1)
                    order = [0, 1, 2] if r == 0 else [3, 2, 1]
                    step = 1 if r == 0 else -1
                    for n, c in enumerate(order):
                        new = STATE[r][:, (c + step) * P:(c + step + 1) * P]
                        kv = KV_BANK[:, c * P:(c + 1) * P]
                        if n == 0:
                            ch.link(dve.tensor_copy(new, kv))
                        else:
                            ins = dve.scalar_tensor_tensor(new, STATE[r][:, c * P:(c + 1) * P], EB[:, c:c + 1], kv,
                                                           ALU.mult, ALU.add)
                            if n == 1:
                                ch.link(ins)
                            else:
                                ins.then_inc(hg_state, 1)
                hold(dve, "dve", hg_o_copied, i + 1)
                ch.link(dve.tensor_tensor(OSQ, OH, OH, ALU.mult))
                ch.link(dve.tensor_reduce(ST[:, 8:12], OSQ.rearrange("p (c d) -> p c d", c=NB), AX.X, ALU.add))
                dve.tensor_scalar(RS[:, 0:4], ST[:, 8:12], 1.0 / P, RMS_EPS, ALU.mult, ALU.add).then_inc(hg_ms, 1)
                hold(dve, "dve", hg_std, i + 1)
                ch.link(dve.reciprocal(ST[:, 0:4], RS[:, 0:4]))
                for c in range(NB):
                    o = OH[:, c * P:(c + 1) * P]
                    ch.link(dve.scalar_tensor_tensor(o, o, ST[:, c:c + 1], HROWN[:, :], ALU.mult, ALU.mult))
                    dve.tensor_tensor(o, o, tm(Y, 12, T, c, i * P, P), ALU.mult).then_inc(hg_normed, 1)

            ch.loop(HG_HEADS, 2 * (1 + 1 + 1 + 1 + 2) + 3 + NB, recurrence)
            for b in range(NB):
                dve.wait_ge(bank_free, POS["up"] + 8 + 2 * b + 2 + 4)
                rec = tm(H, 0, D, b)
                ch.link(dve.tensor_tensor(rec, rec, G[:, b * 2048 + D:(b + 1) * 2048], ALU.mult))
                dve.wait_ge(merged, b + 1)
                ins = dve.tensor_tensor(tm(MKF, 0, D, b), tm(MKF, 0, D, b), rec, ALU.add)
                if b < NB - 1:
                    ch.link(ins)
            ins.then_inc(up_gated, 1)
            dve.wait_ge(bank_free, POS["out_c"] + 8 + 4)
            for b in range(NB):
                ch.link(dve.tensor_tensor(X[:, b, :], X[:, b, :], tm(H, 0, D, b), ALU.add))
            ch.link(rms_rows(7))
            dve.wait_ge(loaded_rows, 32 * 2 + 16)
            for b in range(NB):
                ins = dve.tensor_tensor(tm(H, 0, D, b), tm(H, 0, D, b), ROW[:, 0, :], ALU.mult)
                if b < NB - 1:
                    ch.link(ins)
            ins.then_inc(h_ready, 1)
            dve.memset(ZERO[:, :], 0.0).then_inc(zero_ready, 1)
            dve.wait_ge(bank_free, POS["sk"] + 16 + 4)
            dve.wait_ge(h_ready, 1)

            shape = [P, 16, 16]

            def first(a):
                return a.rearrange("p (k o) -> p k o", o=1).broadcast_to(shape)

            def second(a):
                return a.rearrange("p (o k) -> p o k", o=1).broadcast_to(shape)

            def square(a):
                return a.rearrange("p (i j) -> p i j", i=16)

            def top16_step(n, values, val, idx):
                half = slice(0, 8) if n < 3 else slice(8, 16)
                if n in (0, 3):
                    ch.link(dve.max(val[:, half], values))
                elif n in (1, 4):
                    ch.link(dve.max_index(idx[:, half], val[:, half], values))
                else:
                    ch.link(dve.match_replace(values, val[:, half], values, TAKEN))

            def route_step(g, k):
                if k == 0:
                    ch.link(dve.tensor_copy(WS, Y[:, ds(g * 256, 256)]))
                if k < 5:
                    for q in range(2):
                        top16_step(k, WS[:, q * P:(q + 1) * P], TOPV[:, q * 16:q * 16 + 16],
                                   TOPI[:, q * 16:q * 16 + 16])
                if k == 5:
                    ch.link(dve.tensor_copy(TOPF, TOPI))
                    ch.link(dve.tensor_tensor(square(CAND), first(TOPV[:, 0:16]), second(TOPV[:, 16:32]), ALU.add))
                if 6 <= k < 11:
                    top16_step(k - 6, CAND, BEST, BESTI)
                if k == 11:
                    ch.link(dve.tensor_scalar(PARTI[:, 0:16], BESTI, 4, None, ALU.logical_shift_right))
                    ch.link(dve.tensor_scalar(PARTI[:, 16:32], BESTI, 15, None, ALU.bitwise_and))
                    ch.link(dve.tensor_copy(PARTF, PARTI))
                if k in (12, 13):
                    a = k - 12
                    rank = C[:, CC["iota"]:CC["iota"] + 16]
                    ch.link(dve.tensor_tensor(square(HOT), first(PARTF[:, a * 16:a * 16 + 16]), second(rank),
                                              ALU.is_equal))
                    ch.link(dve.tensor_tensor(square(HOT), square(HOT), second(TOPF[:, a * 16:a * 16 + 16]), ALU.mult))
                    ch.link(dve.tensor_reduce(PICK[:, a * 16:a * 16 + 16], square(HOT), AX.X, ALU.add))
                if k == 14:
                    ch.link(dve.scalar_tensor_tensor(PICK[:, 0:16], PICK[:, 0:16], float(P), PICK[:, 16:32],
                                                     ALU.mult, ALU.add))
                if k == 15:
                    dve.tensor_scalar(GW[:, ds(g * 16, 16)], BEST, BEST[:, 0:1], None, ALU.subtract)
                    dve.tensor_copy(IDX[:, ds(g * 16, 16)], PICK[:, 0:16]).then_inc(picked, 1)
                    hold(dve, "dve", picked, g + 1)

            ROUTE_LINKS = 1 + 10 + 2 + 5 + 3 + 6 + 1

            def wait_dve(semaphore, value):
                if isinstance(value, int):
                    dve.wait_ge(semaphore, value)
                else:
                    hold(dve, "dve", semaphore, value)

            def weigh(g, s, ahead):
                for k in range(PEER_K):
                    wait_dve(u_loaded[k % RING], g * 64 + 16 * (k // RING + 1))
                    wait_dve(dots, g * 16 + k + 15)
                    dve.tensor_tensor_reduce(out=JUNK[k % 2], in0=UB[k % RING], in1=HC, scale=1.0, scalar=0.0,
                                             op0=ALU.mult, op1=ALU.add, accum_out=AA[s][:, k:k + 1]
                                             ).then_inc(dots, 1)
                    if ahead:
                        route_step(g + 2, k)
                wait_dve(dots, g * 16 + 32)
                a = AA[s]
                ch.link(dve.tensor_tensor(GT, a, a, ALU.mult))
                ch.link(dve.tensor_scalar(GT, GT, 0.044715, 1.0, ALU.mult, ALU.add))
                dve.tensor_tensor(GT, GT, a, ALU.mult).then_inc(tanh_in, 1)
                wait_dve(tanh_out, g + 1)
                dve.reciprocal(RSUM, SUMS)
                ch.link(dve.scalar_tensor_tensor(TH, TH, 1.0, a, ALU.add, ALU.mult))
                ch.link(dve.tensor_scalar(TH, TH, RSUM, 0.5, ALU.mult, ALU.mult))
                dve.tensor_tensor(WV[s], TH, EXPS, ALU.mult).then_inc(weights, 1)

            WEIGH_LINKS = 4

            def two_groups(i, ahead):
                ch.link(dve.tensor_copy(HC, H[:, ds((i // (PEER_HEADS // 2)) * D, D)]))
                for s in range(2):
                    weigh(i * 2 + s, s, ahead)

            dve.sem_inc(dots, 16)

            def route(g):
                for k in range(PEER_K):
                    route_step(g, k)

            ch.loop(2, ROUTE_LINKS, route)
            ch.loop(GROUPS // 2 - 1, 1 + 2 * (ROUTE_LINKS + WEIGH_LINKS), lambda i: two_groups(i, True))
            two_groups(GROUPS // 2 - 1, False)
            dve.wait_ge(acc_free, 1 + NB)
            for b in range(NB):
                ch.link(dve.tensor_tensor(X[:, b, :], X[:, b, :], tm(Y, 0, D, b), ALU.add))
            rms_rows(8).then_inc(xn_ready, 1)
            dve.wait_ge(bank_free, POS["end"] + 4)
            for b in range(NB):
                ch.link(dve.tensor_tensor(tm(G, 0, D, b), tm(G, 0, D, b), tm(Y, 0, D, b), ALU.mult))
                ins = dve.tensor_tensor(X[:, b, :], X[:, b, :], tm(G, 0, D, b), ALU.add)
                if b < NB - 1:
                    ch.link(ins)
            ins.then_inc(y_ready, 1)


def shape_constants():
    q, m = np.arange(P)[:, None], np.arange(896)[None, :]
    dist = np.abs(q - (m - 384))
    adm = np.where(np.arange(P)[None, :] // CHUNK <= q // CHUNK, 0.0, NEG)
    base = [2.0 ** (-8.0 * (i + 1) / 8) for i in range(8)]
    extra = [2.0 ** (-4.0 * (2 * i + 1) / 8) for i in range(HEADS_B - 8)]
    slope = np.broadcast_to(-np.float32(base + extra) / np.float32(SCALE128), (P, HEADS_B))
    t = np.arange(T)
    inv = (10000.0 ** (-np.arange(16, dtype=np.float32) / 16)).astype(np.float32)
    ang = np.stack([(t // 64).astype(np.float32)[:, None] * inv, (t % 64).astype(np.float32)[:, None] * inv], 1)
    table = lambda v: v.reshape(NB, P, 32).transpose(1, 0, 2).reshape(P, -1)
    return np.concatenate([np.eye(P), dist, adm, slope, table(np.cos(ang)), table(np.sin(ang)),
                           np.broadcast_to(np.arange(16), (P, 16))],
                          1).astype(np.float32)


def level_masks():
    s, t = np.arange(P)[:, None], np.arange(P)[None, :]
    fwd = [(s // (2 * m) == t // (2 * m)) & (s % (2 * m) < m) & (t % (2 * m) >= m)
           for m in (64 >> l for l in range(LEVELS))]
    bwd = [a.T for a in fwd]
    return np.concatenate(fwd + bwd, 1).astype(np.float32)


def slots_of(w, n=T):
    s = [w[:, c:c + n].reshape(KD, P, n).transpose(1, 0, 2) for c in range(0, w.shape[1], n)]
    return [a.reshape(P, -1) for a in s]


def out_slots(w):
    return [w[k:k + D, n:n + T].reshape(KD, P, T).transpose(1, 0, 2).reshape(P, -1)
            for n in range(0, w.shape[1], T) for k in range(0, w.shape[0], D)]


def lay_out(i):
    f = lambda v: v.reshape(-1, P).T
    aw, bw = i["a_w_in"][0], i["b_w_in"][0]
    a, gl = slots_of(aw[:, 0:1536]), slots_of(aw[:, 1536:3072])
    w = slots_of(i["a_w_mkv"][0]) + slots_of(i["b_w_mkv"][0])
    w += [s for pair in zip(a, gl) for s in pair]
    w += slots_of(aw[:, 3584:5632]) + slots_of(aw[:, 3072:3584]) + out_slots(i["a_w_out"][0])
    spec = np.concatenate([bw[:, 2048:2304], bw[:, 2304:2368], bw[:, 2304:2368], bw[:, 2368:2376],
                           np.zeros((D, 120), bw.dtype)], 1)
    w += slots_of(bw[:, 0:2048]) + slots_of(spec) + slots_of(bw[:, 2376:2888]) + slots_of(bw[:, 2888:4936])
    w += out_slots(i["b_w_out"][0])
    cw = i["w_in_2"][0]
    akv = np.concatenate([cw[:, 512:768], np.zeros((D, 256), cw.dtype)], 1)
    w += slots_of(cw[:, 0:512]) + slots_of(akv) + slots_of(cw[:, 768:])
    w += [i[n][0].reshape(4, P, D).transpose(1, 0, 2).reshape(P, -1) for n in ("w_up_att_2", "w_up_hg_2")]
    w += slots_of(i["w_out_2"][0]) + slots_of(i["peer_wq_2"][0]) + slots_of(i["ple_gate_2"][0])
    proj = i["ple_proj_2"][0].reshape(2, P, D).transpose(1, 0, 2).reshape(P, -1)
    w.append(np.concatenate([proj, np.zeros_like(proj)], 1))
    sub = i["peer_subkeys_2"][0].reshape(16, P, P).transpose(2, 0, 1).reshape(P, -1)
    norm_rows = np.concatenate([np.tile(i["q_norm_2"][0], 8), np.tile(i["k_norm_2"][0], 2), i["hg_out_norm_2"][0]])
    conv = i["a_conv_w"][0].T.reshape(CONV_T, P, TAPS).transpose(1, 0, 2).reshape(P, -1)
    fmvec = np.concatenate([f(i["mem_ln_g"]), f(i["mem_ln_b"]), f(i["a_conv_b"][0]), f(i["a_ln_g"][0]),
                            f(i["a_ln_b"][0]), conv, f(i["norm_mix_2"][0]), f(i["norm_ple_2"][0]),
                            f(i["hg_lb_raw_2"][0]), f(i["hg_lb_raw_2"][1])], 1)
    rows = np.stack([i["a_post_g"][0], i["a_post_b"][0], i["b_post_g"][0], i["b_post_b"][0],
                     i["norm_ffn_2"][0]])
    return {"x": i["x"][0], "xT": i["x"][0].T, "mem": i["mem"][0], "wstream": np.stack(w), "fmvec": fmvec,
            "rows": rows, "norm_rows": norm_rows, "consts": shape_constants(), "levels": level_masks(),
            "subkeys": sub, "pT": i["p_2"][0, 0].T, "peer_u": i["peer_u_2"][0], "peer_v": i["peer_v_2"][0]}


OUT_SHAPE = (1, T, D)


def kernel(**inputs):
    import concourse.bacc as bacc
    from concourse.bass_utils import run_bass_kernel_spmd as run

    arrays = {k: np.ascontiguousarray(v) for k, v in lay_out({k: np.asarray(v) for k, v in inputs.items()}).items()}
    nc = bacc.Bacc("TRN2", target_bir_lowering=False, num_devices=1)
    args = {k: nc.dram_tensor(k, v.shape, mybir.dt.from_np(v.dtype), kind="ExternalInput").ap()
            for k, v in arrays.items()}
    args["out"] = nc.dram_tensor("out", OUT_SHAPE, F32, kind="ExternalOutput").ap()
    program(nc, **args)
    return run(nc, [arrays], core_ids=[0]).results[0]["out"]
```

```python
from contextlib import ExitStack

import numpy as np
import concourse.bass as bass
from concourse import mybir

F32 = mybir.dt.float32
U32 = mybir.dt.uint32
ALU = mybir.AluOpType
ACT = mybir.ActivationFunctionType
AX = mybir.AxisListType
ds = bass.ds

P = 128
T = 512
NB = T // P
D = 1024
KD = D // P
N_MEM = 256
CHUNK = 64
CONV_W = 1536
CONV_T = CONV_W // P
TAPS = 31
POOL_GATED = 5
HROW = T + TAPS - 1
HEADS_B = 12
IDX_HEADS = 8
TOPK = 128
ALPHA = float(4 ** 0.25)
LN_EPS = 1e-5
RMS_EPS = 1e-6
NEG = -1e30
TAKEN = -3e38
HG_HEADS = 4
LEVELS = 7
ROPE_HEADS = 10
QKV = 768
PEER_HEADS = 8
PEER_K = 16
GROUPS = NB * PEER_HEADS
RING = 4
GELU_C = float(np.sqrt(2 / np.pi))
SCALE128 = float(128 ** -0.5)

SLOTS = {}
POS = {}
UNITS = {}


def _number(table, stages):
    at = 0
    for name, n in stages:
        table[name] = at
        at += n
    table["end"] = at


_number(SLOTS, [("mkv_a", 2), ("mkv_b", 2), ("u", 6), ("gate_a", 4), ("qm_a", 1), ("out_a", 4),
                ("bfm", 4), ("bspec", 1), ("qm_b", 1), ("gate_b", 4), ("out_b", 4),
                ("aq", 1), ("akv", 1), ("hq", 1), ("hff", 1), ("hfb", 1), ("hi", 1), ("hg", 1),
                ("gate_c", 4), ("up", 2), ("out_c", 2), ("wq", 4), ("proj", 1), ("ple", 2)])
_number(POS, [("memT", 8), ("mkv_a", 6), ("mkv_b", 6), ("u", 24), ("gate_a", 16), ("qm_a", 4),
              ("ln", 2), ("out_a", 8), ("xT_a", 8),
              ("bfm", 16), ("bspec", 4), ("vT", 1), ("index", 24), ("qm_b", 4), ("gate_b", 16),
              ("out_b", 8), ("xT_c", 8),
              ("aq", 4), ("akv", 4), ("hq", 4), ("hff", 4), ("hfb", 4), ("hi", 4), ("hg", 4),
              ("gate_c", 16), ("qT", 4), ("kT", 2), ("up", 16), ("mT", 8), ("out_c", 8), ("xT_f", 8),
              ("wq", 32), ("proj", 8), ("xT_p", 8), ("ple", 8)])
_number(UNITS, [("mem_a", 2), ("mem_b", 2), ("dsa", 6), ("gqa", 4)])

FM = {}
_number(FM, [("mem_g", 8), ("mem_b", 8), ("conv_b", 12), ("ln_g", 12), ("ln_b", 12),
             ("conv_w", CONV_T * TAPS), ("mix_g", 8), ("ple_g", 8), ("lb0", 8), ("lb1", 8)])
CC = {}
_number(CC, [("ident", P), ("dist", 896), ("adm", P), ("slope", HEADS_B), ("cos", 128), ("sin", 128), ("iota", 16)])


def program(nc, x, xT, mem, wstream, fmvec, rows, norm_rows, consts, levels, subkeys, pT, peer_u, peer_v, out):
    with ExitStack() as ctx:
        def sb(name, shape, dt=F32):
            return ctx.enter_context(nc.sbuf_tensor(name, shape, dt))

        def sem(name):
            return ctx.enter_context(nc.semaphore(name))

        W = sb("W", [P, 2, 4096])
        X = sb("X", [P, NB, D])
        XT = sb("XT", [P, KD, T])
        G = sb("G", [P, 16 * T])
        Y = sb("Y", [P, 16 * T])
        H = sb("H", [P, 18 * T])
        MK = sb("MK", [P, 2, 2048])
        C = sb("C", [P, CC["end"]])
        V = sb("V", [P, FM["end"]])
        SIG = sb("SIG", [P, 4, T])
        ONES = sb("ONES", [P, P])
        QC = sb("QC", [P, 2, T])
        PR = sb("PR", [P, 2, T])
        WI = sb("WI", [P, NB, IDX_HEADS])
        ST = sb("ST", [P, 64])
        MX2 = sb("MX2", [P, 8])
        MX = sb("MX", [P, 4])
        NM = sb("NM", [P, 4])
        SM = sb("SM", [P, 4])
        RI = sb("RI", [P, 4])
        TOP8 = sb("TOP8", [P, NB - 1, 8])

        ps = [ctx.enter_context(nc.psum_tensor(f"ps{i}", [P, T], F32)) for i in range(8)]
        SC_BANK, PT_BANK, O_BANK = (ps[4], ps[5], ps[0], ps[1], ps[2]), ps[6], (ps[7], ps[3])
        SC = len(SC_BANK)

        ident = C[:, 0:P]
        mem_tm = G[:, 0:2 * D]
        memT = Y[:, 0:KD * N_MEM]
        RES = H[:, 0:NB * D]
        L = SIG
        ROW = SIG[:, :, :].rearrange("p (r a) t -> p r (a t)", r=2)
        MU = PR
        PT = H[:, 14 * T:16 * T].rearrange("p (a t) -> p a t", a=2)
        OS = H[:, 16 * T:18 * T].rearrange("p (a t) -> p a t", a=2)
        VT = H[:, 13 * T:14 * T].rearrange("p (b d) -> p b d", b=NB)
        MB = MK[:, 0, 0:3 * T].rearrange("p (b t) -> p b t", b=3)
        TMP = MK[:, 0, 3 * T:4 * T]

        def tm(region, first, width, b, a=0, n=None):
            n = width - a if n is None else n
            return region[:, ds(first * T + b * width + a, n)]

        MKF = MK[:, :, :].rearrange("p a n -> p (a n)")
        XTF = XT[:, :, :].rearrange("p k t -> p (k t)")
        HQ = SIG
        TMPR = H[:, 13 * T:14 * T]
        QKN = QC[:, :, :].rearrange("p a t -> p (a t)")[:, 0:640]
        KK = PR[:, :, :].rearrange("p a (b c) -> p (a b) c", b=2)
        PLE_P = PR
        HROWN = sb("HROWN", [P, P])
        LB = sb("LB", [P, 8])
        OML = sb("OML", [P, 8])
        EB = sb("EB", [P, 4])
        RS = sb("RS", [P, 40])
        ZERO = sb("ZERO", [P, P])
        KF = [H[:, (0 + r) * T:(1 + r) * T] for r in range(2)]
        BF = [H[:, 2 * T:3 * T], QC[:, 0, :]]
        DD = [H[:, (3 + r) * T:(4 + r) * T] for r in range(2)]
        EE = [H[:, (5 + r) * T:(6 + r) * T] for r in range(2)]
        QE = [H[:, (7 + r) * T:(8 + r) * T] for r in range(2)]
        KE = [H[:, (9 + r) * T:(10 + r) * T] for r in range(2)]
        QB = [H[:, (11 + r) * T:(12 + r) * T] for r in range(2)]
        KDEC = H[:, 13 * T:14 * T]
        AS = [H[:, (14 + r) * T:(15 + r) * T] for r in range(2)]
        STATE = [H[:, (16 + r) * T:(17 + r) * T] for r in range(2)]
        KDT = XTF[:, 4 * T:5 * T]
        OH = XTF[:, 5 * T:6 * T]
        OSQ = XTF[:, 6 * T:7 * T]
        LF = XTF[:, 7 * T:8 * T]
        LVL = XTF[:, 0:2 * LEVELS * P].rearrange("p (r l t) -> p r l t", r=2, l=LEVELS)
        SUB = MKF[:, 0:2048]
        WS = MKF[:, 2048:2304]
        CAND = H[:, 8 * T:8 * T + 256]
        HOT = MKF[:, 2304:2560]
        small = H[:, 9 * T:10 * T]
        TOPV = small[:, 0:32]
        TOPI = small[:, 32:64].bitcast(U32)
        TOPF = small[:, 64:96]
        BEST = small[:, 96:112]
        BESTI = small[:, 112:128].bitcast(U32)
        PARTI = small[:, 128:160].bitcast(U32)
        PARTF = small[:, 160:192]
        PICK = small[:, 192:224]
        EXPS = small[:, 224:240]
        SUMS = small[:, 240:241]
        RSUM = small[:, 241:242]
        IDX = H[:, 14 * T:15 * T].bitcast(U32)
        GW = H[:, 15 * T:16 * T]
        HC = H[:, 16 * T:18 * T]
        UB = [G[:, k * D:(k + 1) * D] for k in range(RING)]
        VB = [G[:, (RING + k) * D:(RING + k + 1) * D] for k in range(RING)]
        JUNK = [MKF[:, 2560:2560 + D], H[:, 10 * T:12 * T]]
        QP = SIG
        DG = [H[:, 12 * T + k * P:12 * T + (k + 1) * P] for k in range(RING)]
        UI = [H[:, 13 * T + a * 16:13 * T + (a + 1) * 16].bitcast(U32) for a in range(2)]
        VI = [H[:, 13 * T + 32 + a * 16:13 * T + 32 + (a + 1) * 16].bitcast(U32) for a in range(2)]
        AA = [H[:, 13 * T + 64 + a * 16:13 * T + 64 + (a + 1) * 16] for a in range(2)]
        WV = [H[:, 13 * T + 96 + a * 16:13 * T + 96 + (a + 1) * 16] for a in range(2)]
        GT = H[:, 13 * T + 128:13 * T + 144]
        TH = H[:, 13 * T + 144:13 * T + 160]
        A_BANK, KV_BANK, HO_BANK = (ps[4], ps[5]), ps[6], ps[7]

        def fm(name, i=0, n=1):
            return V[:, FM[name] + i:FM[name] + i + n]

        def gt(i, n=1):
            return G[:, ds(i * T, n * T)]

        def yt(i, n=1):
            return Y[:, ds(i * T, n * T)]

        def ht(i, n=1):
            return H[:, ds(i * T, n * T)]

        def hrow(i, a, n):
            return H[:, ds(i * HROW + a, n)]

        loaded_x = sem("loaded_x")
        loaded_mem = sem("loaded_mem")
        loaded_const = sem("loaded_const")
        loaded_rows = sem("loaded_rows")
        slot_loaded = [sem("slot_loaded0"), sem("slot_loaded1")]
        slot_used = sem("slot_used")
        bank_full = sem("bank_full")
        bank_free = sem("bank_free")
        passed = {e: sem(f"passed_{e}") for e in ("act", "dve", "pool")}
        dve_link = sem("dve_link")
        act_link = sem("act_link")
        mem_normed = sem("mem_normed")
        glu_free = sem("glu_free")
        glu_done = sem("glu_done")
        conv_tap = sem("conv_tap")
        centred = sem("centred")
        squared = sem("squared")
        squares_used = sem("squares_used")
        scaled = sem("scaled")
        silued = sem("silued")
        mix_gated = sem("mix_gated")
        var_ready = sem("var_ready")
        std_ready = sem("std_ready")
        score_full = sem("score_full")
        score_free = sem("score_free")
        maxed = sem("maxed")
        probs_full = sem("probs_full")
        pT_full = sem("pT_full")
        pT_copied = sem("pT_copied")
        pv_full = sem("pv_full")
        o_free = sem("o_free")
        os_free = sem("os_free")
        q_full = sem("q_full")
        att_gated = sem("att_gated")
        x_normed = sem("x_normed")
        relu_free = sem("relu_free")
        ones_ready = sem("ones_ready")
        loaded_qkn = sem("loaded_qkn")
        loaded_levels = sem("loaded_levels")
        loaded_sub = sem("loaded_sub")
        loaded_p = sem("loaded_p")
        xn_ready = sem("xn_ready")
        qk_part = sem("qk_part")
        rope_done = sem("rope_done")
        kk_ready = sem("kk_ready")
        q_cleared = sem("q_cleared")
        lb_diff = sem("lb_diff")
        lb_sig = sem("lb_sig")
        hg_f = sem("hg_f")
        hg_lf = sem("hg_lf")
        hg_diff = sem("hg_diff")
        hg_exp = sem("hg_exp")
        hg_exp_used = sem("hg_exp_used")
        hg_qe = sem("hg_qe")
        hg_ke = sem("hg_ke")
        hg_a_full = sem("hg_a_full")
        hg_a_free = sem("hg_a_free")
        hg_kdec = sem("hg_kdec")
        hg_qb = sem("hg_qb")
        hg_decay = sem("hg_decay")
        hg_kT_full = sem("hg_kT_full")
        hg_kT_copied = sem("hg_kT_copied")
        hg_kv_full = sem("hg_kv_full")
        hg_state = sem("hg_state")
        hg_o_full = sem("hg_o_full")
        hg_o_copied = sem("hg_o_copied")
        hg_ms = sem("hg_ms")
        hg_std = sem("hg_std")
        hg_normed = sem("hg_normed")
        hg_oT_full = sem("hg_oT_full")
        hg_y = sem("hg_y")
        up_gated = sem("up_gated")
        merged = sem("merged")
        h_ready = sem("h_ready")
        picked = sem("picked")
        staged = sem("staged")
        u_loaded = [sem(f"u_loaded{k}") for k in range(RING)]
        v_loaded = [sem(f"v_loaded{k}") for k in range(RING)]
        sk_ready = sem("sk_ready")
        dots = sem("dots")
        v_done = sem("v_done")
        tanh_in = sem("tanh_in")
        tanh_out = sem("tanh_out")
        weights = sem("weights")
        diag_full = sem("diag_full")
        acc_full = sem("acc_full")
        acc_free = sem("acc_free")
        zero_ready = sem("zero_ready")
        y_ready = sem("y_ready")
        stored = sem("stored")

        def hold(eng, name, semaphore, value):
            eng.wait_ge(semaphore, value)
            eng.sem_inc(passed[name], 1)

        class Chain:

            def __init__(self, eng, name, semaphore):
                self.eng, self.name, self.sem, self.n, self.off = eng, name, semaphore, 0, 0

            def count(self, ins):
                self.n += 1
                ins.then_inc(self.sem, 1)
                return self.n

            def after(self, n):
                if isinstance(self.off, int):
                    self.eng.wait_ge(self.sem, n)
                else:
                    hold(self.eng, self.name, self.sem, self.off + n)

            def link(self, ins):
                self.after(self.count(ins))

            def loop(self, times, per, body):
                base = self.n
                with self.eng.Fori(0, times) as i:
                    self.off = i * per
                    body(i)
                    assert self.n - base == per, (self.n - base, per)
                self.n, self.off = base + times * per, 0

        block = ctx.enter_context(nc.Block())

        @block.sync
        def _(sp):
            sp.dma_start(mem_tm.rearrange("p (b d) -> p b d", b=2),
                         mem.rearrange("(b p) d -> p b d", p=P)).then_inc(loaded_mem, 16)
            sp.dma_start(C[:, :], consts).then_inc(loaded_const, 16)
            sp.dma_start(HROWN[:, :], norm_rows[640:768].partition_broadcast(P)).then_inc(loaded_const, 16)
            sp.dma_start(V[:, :], fmvec).then_inc(loaded_const, 16)
            for s in range(2):
                sp.dma_start(W[:, s, :], wstream[s]).then_inc(slot_loaded[s], 16)
            sp.dma_start(XT[:, :, :], xT.rearrange("(k p) t -> p k t", p=P)).then_inc(loaded_x, 16)
            sp.dma_start(X[:, :, :], x.rearrange("(b p) d -> p b d", p=P)).then_inc(loaded_x, 16)
            n = SLOTS["end"]
            with sp.Fori(1, n // 2) as i:
                for s in range(2):
                    sp.wait_ge(slot_used, i * 2 + s - 1)
                    sp.dma_start(W[:, s, :], wstream[ds(i * 2 + s, 1)].rearrange("a p n -> (a p) n")
                                 ).then_inc(slot_loaded[s], 16)
            if n % 2:
                sp.wait_ge(slot_used, n - 2)
                sp.dma_start(W[:, 0, :], wstream[n - 1]).then_inc(slot_loaded[0], 16)
            for b in range(NB):
                sp.wait_ge(y_ready, b + 1)
                sp.dma_start(out[0, b * P:(b + 1) * P, :], X[:, b, :]).then_inc(stored, 16)
            sp.wait_ge(stored, 16 * NB)

        @block.tensor
        def _(pe):
            def bank(pos):
                pe.wait_ge(bank_free, pos + 1)

            def slot(s0, j, i=None):
                s = s0 + j
                pe.wait_ge(slot_loaded[s % 2], 16 * (s // 2 + 1) + (0 if i is None else i * 16))
                return W[:, s % 2, :]

            def project_fm(w, pos0, j, i_pos, rhs, tiles=4):
                w = w.rearrange("p (k n) -> p k n", k=KD)
                for m in range(tiles):
                    bank(i_pos + (pos0 + 4 * j + m))
                    b = ps[(pos0 + m) % 4]
                    for k in range(KD):
                        mm = pe.matmul(b[:, 0:rhs[k].shape[-1]], w[:, k, m * P:(m + 1) * P], rhs[k],
                                       start=(k == 0), stop=(k == KD - 1))
                    mm.then_inc(bank_full, 1)

            def used():
                pe.drain().then_inc(slot_used, 1)

            def stage_fm(name, i=None, slots=2):
                for j in range(slots):
                    w = slot(SLOTS[name], j, i)
                    project_fm(w, POS[name], j, 0 if i is None else i * 4 * slots,
                               [XT[:, k, :] for k in range(KD)])
                    used()

            def mem_kv(name):
                w = slot(SLOTS[name], 0)
                mt = memT.rearrange("p (k n) -> p k n", k=KD)
                project_fm(w, POS[name], 0, 0, [mt[:, k, :] for k in range(KD)])
                used()
                w = slot(SLOTS[name], 1).rearrange("p (k n) -> p k n", k=KD)
                for b in range(2):
                    pos = POS[name] + 4 + b
                    bank(pos)
                    for k in range(KD):
                        mm = pe.matmul(ps[pos % 4][:, :], mt[:, k, b * P:(b + 1) * P], w[:, k, :],
                                       start=(k == 0), stop=(k == KD - 1))
                    mm.then_inc(bank_full, 1)
                used()

            def transposes(pos, parts):
                bank(pos)
                for n, src in enumerate(parts):
                    mm = pe.transpose(ps[pos % 4][:, n * P:(n + 1) * P], src, ident)
                mm.then_inc(bank_full, 1)

            def attention(name, times, unit0, n_keys, k_of, v_of, dv, joined=False):
                with pe.Fori(0, times) as i:
                    place = 0

                    def score_bank():
                        nonlocal place
                        b = SC_BANK[place % SC]
                        pe.wait_ge(score_free, (unit0 + i) * 10 + place + 1)
                        place += 1
                        return b

                    for t in range(-1, 11):
                        if t < 7:
                            e, b = (t + 1) // 4, (t + 1) % 4
                            if b == 0:
                                pe.wait_ge(q_full, (unit0 + i) * 2 + e + 1)
                            s = score_bank()
                            n = n_keys(b)
                            pe.matmul(s[:, 0:n], QC[:, e, b * P:(b + 1) * P], k_of(i, e, n),
                                      start=True, stop=True).then_inc(score_full, 1)
                        outs = ([0, 1] if t == 10 else []) if joined else {6: [0], 10: [1]}.get(t, [])
                        for e in outs:
                            s = score_bank()
                            pe.wait_ge(o_free, (unit0 + i) * 8 + 2 + (8 if joined else 4 * e + 4))
                            for b in range(2 if joined else 4):
                                mm = pe.transpose(s[:, b * P:(b + 1) * P], OS[:, e, b * P:(b + 1) * P], ident)
                            mm.then_inc(score_full, 1)
                        if 1 <= t <= 8:
                            u = t - 1
                            n = n_keys(u % 4) // P
                            pe.wait_ge(probs_full, (unit0 + i) * 8 + u + 1)
                            pe.wait_ge(pT_copied, (unit0 + i) * 8 + u + 1)
                            for k in range(n):
                                mm = pe.transpose(PT_BANK[:, k * P:(k + 1) * P],
                                                  PR[:, u % 2, k * P:(k + 1) * P], ident)
                            mm.then_inc(pT_full, 1)
                        if 2 <= t <= 9:
                            u = t - 2
                            n = n_keys(u % 4) // P
                            pe.wait_ge(pT_copied, (unit0 + i) * 8 + u + 2)
                            pe.wait_ge(o_free, (unit0 + i) * 8 + u + 1)
                            for k in range(n):
                                mm = pe.matmul(O_BANK[u % 2][:, 0:dv],
                                               PT[:, u % 2, k * P:(k + 1) * P], v_of(i, u // 4, k),
                                               start=(k == 0), stop=(k == n - 1))
                            mm.then_inc(pv_full, 1)

            def mem_attention(name, layer):
                kT = MK[:, layer, 0:1024]
                v = MK[:, layer, 1024:2048]
                attention(name, 2, UNITS[name], lambda b: N_MEM,
                          lambda i, e, n: kT[:, ds(i * 512 + e * 256, 256)],
                          lambda i, e, k: v[:, ds(i * 256 + e * 128 + k * 512, 128)], P)

            def out_projection(name):
                with pe.Fori(0, 2) as i:
                    for j in range(2):
                        w = slot(SLOTS[name], j, i).rearrange("p (k n) -> p k n", k=KD)
                        for b in range(NB):
                            pos = POS[name] + b
                            if j == 0:
                                bank(i * 4 + pos)
                            for k in range(KD):
                                mm = pe.matmul(ps[pos % 4][:, :],
                                               Y[:, (j * KD + k) * T + b * P:(j * KD + k) * T + (b + 1) * P],
                                               w[:, k, :], start=(j == 0 and k == 0),
                                               stop=(j == 1 and k == KD - 1))
                            if j == 1:
                                mm.then_inc(bank_full, 1)
                        used()

            def x_transposes(name, done):
                pe.wait_ge(x_normed, done)
                for k in range(KD):
                    transposes(POS[name] + k, [X[:, b, k * P:(k + 1) * P] for b in range(NB)])

            pe.sem_inc(hg_a_full, 1)
            pe.wait_ge(loaded_const, 48)
            pe.wait_ge(mem_normed, 1)
            for k in range(KD):
                transposes(POS["memT"] + k, [mem_tm[:, b * D + k * P:b * D + (k + 1) * P] for b in range(2)])
            pe.wait_ge(bank_free, POS["mkv_a"] + 4)
            mem_kv("mkv_a")
            mem_kv("mkv_b")
            pe.wait_ge(loaded_x, 32)
            with pe.Fori(0, 3) as i:
                stage_fm("u", i)
            with pe.Fori(0, 2) as i:
                stage_fm("gate_a", i)
            stage_fm("qm_a", None, 1)

            def ring_drained(pos):
                pe.wait_ge(bank_free, pos + 4)

            def scores_drained(units):
                pe.wait_ge(score_free, units * 10 + SC)

            ring_drained(POS["ln"])
            mem_attention("mem_a", 0)
            scores_drained(UNITS["mem_b"])
            pe.wait_ge(conv_tap, CONV_T * TAPS)
            pe.wait_ge(ones_ready, 1)
            pos = POS["ln"]
            bank(pos)
            for c in range(CONV_T):
                mm = pe.matmul(ps[pos % 4][:, :], ONES[:, :], yt(c), start=(c == 0), stop=(c == CONV_T - 1))
            mm.then_inc(bank_full, 1)
            bank(pos + 1)
            for c in range(CONV_T):
                pe.wait_ge(squared, c + 1)
                mm = pe.matmul(ps[(pos + 1) % 4][:, :], ONES[:, :], SIG[:, c % 4, :],
                               start=(c == 0), stop=(c == CONV_T - 1))
                if c < CONV_T - 1:
                    mm.then_inc(squares_used, 1)
            mm.then_inc(bank_full, 1)
            pe.wait_ge(mix_gated, CONV_T)
            pe.wait_ge(att_gated, 4)
            out_projection("out_a")
            x_transposes("xT_a", NB)
            pe.wait_ge(bank_free, POS["bfm"] + 4)
            with pe.Fori(0, 2) as i:
                stage_fm("bfm", i)
            w = slot(SLOTS["bspec"], 0)
            pos = POS["bspec"]
            w3 = w.rearrange("p (k n) -> p k n", k=KD)
            for m in range(3):
                bank(pos + m)
                for k in range(KD):
                    mm = pe.matmul(ps[(pos + m) % 4][:, :], w3[:, k, m * P:(m + 1) * P], XT[:, k, :],
                                   start=(k == 0), stop=(k == KD - 1))
                mm.then_inc(bank_full, 1)
            bank(pos + 3)
            for b in range(NB):
                for k in range(KD):
                    mm = pe.matmul(ps[(pos + 3) % 4][:, b * IDX_HEADS:(b + 1) * IDX_HEADS],
                                   XT[:, k, b * P:(b + 1) * P], w3[:, k, 3 * P:3 * P + IDX_HEADS],
                                   start=(k == 0), stop=(k == KD - 1))
            mm.then_inc(bank_full, 1)
            used()
            pe.wait_ge(bank_free, POS["bfm"] + 14 + 4)
            transposes(POS["vT"], [H[:, 13 * T + b * P:13 * T + (b + 1) * P] for b in range(NB)])
            pe.wait_ge(bank_free, POS["bspec"] + 4 + 4)
            pos = POS["index"]
            for b in range(1, NB):
                for h in range(IDX_HEADS):
                    r = 64 * (h % 2)
                    bank(pos)
                    pe.matmul(ps[pos % 4][:, 0:(b + 1) * P],
                              H[r:r + 64, (14 + h // 2) * T + b * P:(14 + h // 2) * T + (b + 1) * P],
                              QC[r:r + 64, 1, 0:(b + 1) * P],
                              start=True, stop=True).then_inc(bank_full, 1)
                    pos += 1
            stage_fm("qm_b", None, 1)
            with pe.Fori(0, 2) as i:
                stage_fm("gate_b", i)
            ring_drained(POS["out_b"])
            mem_attention("mem_b", 1)
            attention("dsa", 6, UNITS["dsa"], lambda b: (b + 1) * P,
                      lambda i, e, n: H[:, 12 * T:12 * T + n],
                      lambda i, e, k: VT[:, k, :], P)
            scores_drained(UNITS["gqa"])
            pe.wait_ge(att_gated, 4 + 4 + 12)
            out_projection("out_b")
            def normed_transposes(name, src, ready, count):
                pe.wait_ge(ready, count)
                for k in range(KD):
                    transposes(POS[name] + k, [src[:, b * D + k * P:b * D + (k + 1) * P] for b in range(NB)])

            def stage_tm(name, i=None, slots=1, n=T):
                for j in range(slots):
                    w = slot(SLOTS[name], j, i).rearrange("p (k n) -> p k n", k=KD)
                    for b in range(NB):
                        p0 = POS[name] + 4 * j + b
                        bank(p0 if i is None else i * (4 * slots) + p0)
                        for k in range(KD):
                            mm = pe.matmul(ps[p0 % 4][:, 0:n], XT[:, k, b * P:(b + 1) * P], w[:, k, 0:n],
                                           start=(k == 0), stop=(k == KD - 1))
                        mm.then_inc(bank_full, 1)
                    used()

            normed_transposes("xT_c", RES, xn_ready, NB)
            pe.wait_ge(bank_free, POS["aq"] + 4)
            stage_tm("aq")
            stage_tm("akv", n=256)
            stage_fm("hq", None, 1)
            stage_fm("hff", None, 1)
            stage_fm("hfb", None, 1)
            stage_tm("hi")
            stage_tm("hg")
            with pe.Fori(0, 2) as i:
                stage_tm("gate_c", i, 2)
            pe.wait_ge(rope_done, NB)
            for m in range(4):
                transposes(POS["qT"] + m, [H[:, 6 * T + b * 640 + m * P:6 * T + b * 640 + (m + 1) * P]
                                           for b in range(NB)])
            pe.wait_ge(kk_ready, 2)
            for g in range(2):
                transposes(POS["kT"] + g, [KK[:, b, g * P:(g + 1) * P] for b in range(NB)])
            ring_drained(POS["up"])
            attention("gqa", 4, UNITS["gqa"], lambda b: T,
                      lambda i, e, n: H[:, ds(11 * T + (i // 2) * T, T)],
                      lambda i, e, k: tm(H, 0, QKV, k, 640 + (i // 2) * 64, 64), 64, joined=True)

            pe.wait_ge(loaded_levels, 16)
            def direction(i, r):
                unit = i * 2 + r
                for l in range(LEVELS + 1):
                    pe.wait_ge(hg_a_free, unit * 8 + l + 1)
                    if l < LEVELS:
                        pe.wait_ge(hg_ke, unit * LEVELS + l + 2)
                        pe.wait_ge(hg_qe, unit * LEVELS + l + 1)
                        ke = KE[l % 2]
                    else:
                        ke = KF[r]
                    for c in range(NB):
                        rhs = (QE[l % 2][:, c * P:(c + 1) * P] if l < LEVELS else
                               HQ[:, :, :].rearrange("p h t -> p (h t)")[:, ds(i * T + c * P, P)])
                        mm = pe.matmul(A_BANK[l % 2][:, c * P:(c + 1) * P], ke[:, c * P:(c + 1) * P], rhs,
                                       start=True, stop=True)
                    mm.then_inc(hg_a_full, 1)
                pe.wait_ge(hg_kdec, unit + 1)
                pe.wait_ge(hg_state, unit + 1)
                for c in range(NB):
                    mm = pe.transpose(KV_BANK[:, c * P:(c + 1) * P], KDEC[:, c * P:(c + 1) * P], ident)
                mm.then_inc(hg_kT_full, 1)
                pe.wait_ge(hg_kT_copied, unit + 1)
                for c in (range(3) if r == 0 else range(1, 4)):
                    mm = pe.matmul(KV_BANK[:, c * P:(c + 1) * P], KDT[:, c * P:(c + 1) * P],
                                   tm(Y, 8, T, c, i * P, P), start=True, stop=True)
                mm.then_inc(hg_kv_full, 1)

            def head_outputs(i):
                pe.wait_ge(hg_state, i * 2 + 3)
                pe.wait_ge(hg_y, i + 1)
                pe.wait_ge(hg_a_free, i * 16 + 16 + 2)
                for c in range(NB):
                    v = tm(Y, 8, T, c, i * P, P)
                    parts = [(AS[0][:, c * P:(c + 1) * P], v), (AS[1][:, c * P:(c + 1) * P], v)]
                    if c > 0:
                        parts.append((QB[0][:, c * P:(c + 1) * P], STATE[0][:, c * P:(c + 1) * P]))
                    if c < NB - 1:
                        parts.append((QB[1][:, c * P:(c + 1) * P], STATE[1][:, c * P:(c + 1) * P]))
                    for n, (a, b) in enumerate(parts):
                        mm = pe.matmul(HO_BANK[:, c * P:(c + 1) * P], a, b, start=(n == 0),
                                       stop=(n == len(parts) - 1))
                mm.then_inc(hg_o_full, 1)

            def outputs_transposed(i):
                pe.wait_ge(hg_normed, i * NB + NB)
                for c in range(NB):
                    mm = pe.transpose(HO_BANK[:, c * P:(c + 1) * P], OH[:, c * P:(c + 1) * P], ident)
                mm.then_inc(hg_oT_full, 1)

            direction(0, 0)
            with pe.Fori(0, HG_HEADS - 1) as i:
                direction(i, 1)
                head_outputs(i)
                direction(i + 1, 0)
                outputs_transposed(i)
            direction(HG_HEADS - 1, 1)
            head_outputs(HG_HEADS - 1)
            outputs_transposed(HG_HEADS - 1)
            pe.wait_ge(hg_y, HG_HEADS + 1)
            for j in range(2):
                w = slot(SLOTS["up"], j).rearrange("p (k n) -> p k n", k=4)
                for b in range(NB):
                    for n in range(2):
                        pos = POS["up"] + 8 * j + 2 * b + n
                        bank(pos)
                        for k in range(4):
                            c0 = (4 * j + k) * T + b * P
                            mm = pe.matmul(ps[pos % 4][:, :], Y[:, c0:c0 + P], w[:, k, n * T:(n + 1) * T],
                                           start=(k == 0), stop=(k == 3))
                        mm.then_inc(bank_full, 1)
                used()
            normed_transposes("mT", MKF, up_gated, 1)
            pe.wait_ge(bank_free, POS["out_c"] + 4)
            stage_tm("out_c", None, 2)
            normed_transposes("xT_f", RES, h_ready, NB)
            pe.wait_ge(bank_free, POS["wq"] + 4)
            pe.wait_ge(loaded_sub, 16)
            pe.sem_inc(v_done, 17)
            with pe.Fori(0, 2) as i:
                for j in range(2):
                    w = slot(SLOTS["wq"], j, i)
                    project_fm(w, POS["wq"], 2 * j, i * 16, [XT[:, k, :] for k in range(KD)])
                    used()
                    pe.wait_ge(bank_free, i * 16 + (POS["wq"] + 8 * j + 4 + 4))
                    for b in range(NB):
                        pos = POS["wq"] + 8 * j + 4 + b
                        bank(i * 16 + pos)
                        for n in range(4):
                            mm = pe.matmul(ps[pos % 4][:, n * P:(n + 1) * P], QP[:, n, b * P:(b + 1) * P],
                                           SUB[:, ds(i * (8 * P) + (4 * j + n) * P, P)], start=True, stop=True)
                        mm.then_inc(bank_full, 1)
            pe.wait_ge(zero_ready, 1)
            pe.wait_ge(bank_free, POS["wq"] + 32 + 4)
            with pe.Fori(0, NB) as b:
                pe.wait_ge(acc_free, b + 1)
                for n in range(2):
                    pe.matmul(ps[n][:, :], ZERO[:, :], C[:, 0:T], start=True, stop=False, skip_group_check=True)
                with pe.Fori(0, PEER_HEADS // 2) as j:
                    for s in range(2):
                        g = b * PEER_HEADS + j * 2 + s
                        for k in range(PEER_K):
                            pe.wait_ge(v_loaded[k % RING], g * 64 + 16 * (k // RING + 1))
                            pe.wait_ge(diag_full, g * 16 + k + 1)
                            for n in range(2):
                                mm = pe.matmul(ps[n][:, :], DG[k % RING], VB[k % RING][:, n * T:(n + 1) * T],
                                               start=False, stop=False, skip_group_check=True)
                            mm.then_inc(v_done, 1)
                for n in range(2):
                    mm = pe.matmul(ps[n][:, :], ZERO[:, :], C[:, 0:T], start=False, stop=True,
                                   skip_group_check=True)
                mm.then_inc(acc_full, 1)
            pe.wait_ge(acc_free, 1 + NB)
            pe.wait_ge(loaded_p, 16)
            w = slot(SLOTS["proj"], 0).rearrange("p (k n) -> p k n", k=4)
            for b in range(NB):
                for n in range(2):
                    pos = POS["proj"] + 2 * b + n
                    bank(pos)
                    for k in range(2):
                        mm = pe.matmul(ps[pos % 4][:, :], PLE_P[:, k, b * P:(b + 1) * P], w[:, k, n * T:(n + 1) * T],
                                       start=(k == 0), stop=(k == 1))
                    mm.then_inc(bank_full, 1)
            used()
            normed_transposes("xT_p", RES, xn_ready, NB + 1)
            pe.wait_ge(bank_free, POS["ple"] + 4)
            stage_tm("ple", None, 2)

        @block.scalar
        def _(act):
            act.sem_inc(bank_free, 4)
            act.sem_inc(score_free, SC)
            act.sem_inc(os_free, 2)
            act.sem_inc(pT_copied, 1)
            act.sem_inc(hg_y, 1)
            ac = Chain(act, "act", act_link)

            def drain(pos, emit, i=None, per=0):
                if i is None:
                    act.wait_ge(bank_full, pos + 1)
                else:
                    hold(act, "act", bank_full, i * per + pos + 1)
                emit(ps[pos % 4]).then_inc(bank_free, 1)

            def copy_to(dst, n=T):
                return lambda b: act.activation(dst, b[:, 0:n], ACT.Copy)

            def mem_kv(name, layer):
                for m in range(4):
                    drain(POS[name] + m, copy_to(MK[:, layer, m * 256:(m + 1) * 256], 256))
                for b in range(2):
                    drain(POS[name] + 4 + b, copy_to(MK[:, layer, 1024 + b * T:1024 + (b + 1) * T]))

            def attention(name, times, biased, n_keys, scale, dst, joined=False):
                unit0 = UNITS[name]
                with act.Fori(0, times) as i:
                    place = 0

                    def scores():
                        nonlocal place
                        hold(act, "act", score_full, (unit0 + i) * 10 + place + 1)
                        place += 1
                        return SC_BANK[(place - 1) % SC]

                    for t in range(11):
                        if t < 8:
                            n = n_keys(t % 4)
                            s = scores()
                            hold(act, "act", maxed, (unit0 + i) * 8 + t + 1)
                            src = L[:, t % 4, 0:n] if biased else s[:, 0:n]
                            act.activation(PR[:, t % 2, 0:n], src, ACT.Exp, bias=NM[:, t % 4:t % 4 + 1],
                                           scale=1.0 if biased else scale,
                                           accum_out=SM[:, t % 4:t % 4 + 1]).then_inc(probs_full, 1)
                            act.sem_inc(passed["act"], 1)
                            hold(act, "act", probs_full, (unit0 + i) * 8 + t + 1)
                            act.sem_inc(score_free, 1)
                        outs = ([0, 1] if t == 10 else []) if joined else {7: [0], 10: [1]}.get(t, [])
                        for e in outs:
                            s = scores()
                            act.activation(dst(i, e), s[:, 0:T // 2 if joined else T], ACT.Copy
                                           ).then_inc(score_free, 1)
                            hold(act, "act", score_free, (unit0 + i) * 10 + place + SC)
                            act.sem_inc(os_free, 1)
                        if 1 <= t <= 8:
                            u = t - 1
                            n = n_keys(u % 4)
                            hold(act, "act", pT_full, (unit0 + i) * 8 + u + 1)
                            act.activation(PT[:, u % 2, 0:n], PT_BANK[:, 0:n], ACT.Copy).then_inc(pT_copied, 1)

            def block_root(b, n):
                act.wait_ge(var_ready, n)
                act.activation(ST[:, 4 + b:5 + b], ST[:, 4 + b:5 + b], ACT.Sqrt).then_inc(std_ready, 1)

            def out_projection(name, n, roots=1):
                for half in range(2):
                    for b in range(NB):
                        drain(POS[name] + 4 * half + b, copy_to(RES[:, b * D + half * T:b * D + (half + 1) * T]))
                        if half == 1:
                            for _ in range(roots):
                                n += 1
                                block_root(b, n)

            def x_transposes(name):
                for k in range(KD):
                    drain(POS[name] + k, copy_to(XT[:, k, :]))

            def load_rows(layer):
                for r in range(2):
                    act.dma_start(ROW[:, r, :], rows[2 * layer + r].partition_broadcast(P)
                                  ).then_inc(loaded_rows, 16)

            act.wait_ge(var_ready, 1)
            act.activation(ST[:, 4:6], ST[:, 4:6], ACT.Sqrt).then_inc(std_ready, 1)
            act.wait_ge(loaded_const, 48)
            for k in range(KD):
                drain(POS["memT"] + k, lambda b: act.activation(
                    memT[:, k * N_MEM:(k + 1) * N_MEM], b[:, 0:N_MEM], ACT.Identity,
                    bias=fm("mem_b", k), scale=fm("mem_g", k)))
            mem_kv("mkv_a", 0)
            mem_kv("mkv_b", 1)
            with act.Fori(0, 3) as i:
                for j in range(4):
                    drain(POS["u"] + j, lambda b: act.activation(hrow(i * 4 + j, TAPS - 1, T), b[:, :], ACT.Copy),
                          i, 8)
                for j in range(4):
                    hold(act, "act", glu_free, i * 4 + j + 1)
                    drain(POS["u"] + 4 + j, lambda b: act.activation(SIG[:, j, :], b[:, :], ACT.Sigmoid), i, 8)
            with act.Fori(0, 2) as i:
                for j in range(8):
                    drain(POS["gate_a"] + j, lambda b: act.activation(gt(i * 8 + j), b[:, :], ACT.Silu), i, 8)
            for j in range(4):
                drain(POS["qm_a"] + j, copy_to(yt(12 + j)))
            attention("mem_a", 2, False, lambda b: N_MEM, SCALE128, lambda i, e: yt(i * 2 + (e + 12)))
            drain(POS["ln"], lambda b: act.activation(MU[:, 0, :], b[:, :], ACT.Copy, scale=1.0 / CONV_W))
            for c in range(CONV_T):
                act.wait_ge(centred, c + 1)
                if c >= 4:
                    act.wait_ge(squares_used, c - 3)
                act.activation(SIG[:, c % 4, :], yt(c), ACT.Square).then_inc(squared, 1)
            drain(POS["ln"] + 1, lambda b: act.activation(MU[:, 1, :], b[:, :], ACT.Copy, scale=1.0 / CONV_W))
            act.wait_ge(var_ready, 2)
            act.activation(MU[:, 1, :], MU[:, 1, :], ACT.Sqrt).then_inc(std_ready, 1)
            load_rows(0)
            for c in range(CONV_T):
                act.wait_ge(scaled, c + 1)
                act.activation(yt(c), yt(c), ACT.Silu, bias=fm("ln_b", c), scale=fm("ln_g", c)
                               ).then_inc(silued, 1)
            out_projection("out_a", 2)
            x_transposes("xT_a")
            with act.Fori(0, 2) as i:
                for j in range(8):
                    drain(POS["bfm"] + j, lambda b: act.activation(ht(i * 8 + j), b[:, :], ACT.Copy), i, 8)
            for m in range(2):
                drain(POS["bspec"] + m, copy_to(ht(16 + m)))
            drain(POS["bspec"] + 2, copy_to(QC[:, 1, :]))
            drain(POS["bspec"] + 3, copy_to(WI[:, :, :].rearrange("p b h -> p (b h)"), NB * IDX_HEADS))
            drain(POS["vT"], copy_to(VT[:, :, :].rearrange("p b d -> p (b d)")))
            pos = POS["index"]
            for b in range(1, NB):
                for h in range(IDX_HEADS):
                    act.wait_ge(relu_free, pos - POS["index"] + 1)
                    drain(pos, lambda bk: act.activation(SIG[:, h % 4, 0:(b + 1) * P], bk[:, 0:(b + 1) * P], ACT.Relu))
                    pos += 1
            for j in range(4):
                drain(POS["qm_b"] + j, copy_to(yt(12 + j)))
            with act.Fori(0, 2) as i:
                for j in range(8):
                    drain(POS["gate_b"] + j, lambda b: act.activation(gt(i * 8 + j), b[:, :], ACT.Silu), i, 8)
            attention("mem_b", 2, False, lambda b: N_MEM, SCALE128, lambda i, e: yt(i * 2 + (e + 12)))
            attention("dsa", 6, True, lambda b: (b + 1) * P, SCALE128, lambda i, e: yt(i * 2 + e))
            load_rows(1)
            out_projection("out_b", 6, 2)
            act.dma_start(QKN, norm_rows[0:640].partition_broadcast(P)).then_inc(loaded_qkn, 16)
            act.wait_ge(lb_diff, 1)
            act.activation(LB[:, :], LB[:, :], ACT.Sigmoid).then_inc(lb_sig, 1)

            def scaled_transposes(name, g):
                for k in range(KD):
                    drain(POS[name] + k, lambda b: act.activation(XT[:, k, :], b[:, :], ACT.Copy, scale=fm(g, k))
                          if g else act.activation(XT[:, k, :], b[:, :], ACT.Copy))

            scaled_transposes("xT_c", "mix_g")
            for b in range(NB):
                drain(POS["aq"] + b, copy_to(tm(H, 0, QKV, b, 0, T)))
            for b in range(NB):
                drain(POS["akv"] + b, copy_to(tm(H, 0, QKV, b, T, 256), 256))
            act.wait_ge(var_ready, 15)
            act.activation(RS[:, :], RS[:, :], ACT.Sqrt).then_inc(std_ready, 1)
            for m in range(4):
                drain(POS["hq"] + m, lambda b: act.activation(HQ[:, m, :], b[:, :], ACT.Silu))
            for m in range(8):
                drain(POS["hff"] + m, lambda b: act.activation(MKF[:, m * T:(m + 1) * T], b[:, :], ACT.Sigmoid))
            for b in range(NB):
                drain(POS["hi"] + b, copy_to(tm(Y, 8, T, b)))
            for b in range(NB):
                drain(POS["hg"] + b, lambda bk: act.activation(tm(Y, 12, T, b), bk[:, :], ACT.Silu))
            with act.Fori(0, 2) as i:
                for j in range(2):
                    for b in range(NB):
                        drain(POS["gate_c"] + 4 * j + b, lambda bk: act.activation(
                            G[:, ds(b * 2048 + i * D + j * T, T)], bk[:, :], ACT.Sigmoid), i, 8)
            act.dma_start(XTF[:, 0:2 * LEVELS * P], levels).then_inc(loaded_levels, 16)
            for m in range(4):
                drain(POS["qT"] + m, copy_to(yt(m)))
            for g in range(2):
                drain(POS["kT"] + g, copy_to(ht(11 + g)))
            attention("gqa", 4, False, lambda b: T, 0.125,
                      lambda i, e: Y[:, ds(i * T + e * (T // 2), T // 2)], joined=True)
            act.dma_start(PLE_P[:, :, :], pT.rearrange("(k p) t -> p k t", p=P)).then_inc(loaded_p, 16)
            def log_gates(i, r):
                hold(act, "act", hg_f, i * 2 + r + 1)
                act.activation(LF, MKF[:, ds(i * T + r * (4 * T), T)], ACT.Ln).then_inc(hg_lf, 1)

            def head_outputs(i):
                hold(act, "act", hg_o_full, i + 1)
                act.activation(OH, HO_BANK[:, :], ACT.Copy)
                for c in range(NB):
                    ins = act.activation(OSQ[:, c * P:(c + 1) * P], HO_BANK[:, c * P:(c + 1) * P], ACT.Square,
                                         accum_out=ST[:, 8 + c:9 + c])
                ins.then_inc(hg_o_copied, 1)

            def output_roots(i):
                hold(act, "act", hg_ms, i + 1)
                act.activation(RS[:, 0:4], RS[:, 0:4], ACT.Sqrt).then_inc(hg_std, 1)

            def outputs_transposed(i):
                hold(act, "act", hg_oT_full, i + 1)
                act.activation(yt(i + 4), HO_BANK[:, :], ACT.Copy).then_inc(hg_y, 1)

            def direction(i, r, following, before=None):
                unit = i * 2 + r
                for l in range(9):
                    hold(act, "act", hg_exp_used, unit * 9 + max(l - 1, 0) + 1)
                    hold(act, "act", hg_ke, unit * LEVELS + min(max(l - 1, 0), LEVELS) + 1)
                    if l < 8:
                        hold(act, "act", hg_diff, unit * 8 + l + 1)
                    if l < LEVELS:
                        m = 64 >> l
                        d = DD[l % 2].rearrange("p (b h m) -> p b h m", h=2, m=m)
                        e = EE[l % 2].rearrange("p (b h m) -> p b h m", h=2, m=m)
                        act.activation(e[:, :, 0, :], d[:, :, 0, :], ACT.Exp, scale=-1.0 if r == 0 else 1.0)
                        ins = act.activation(e[:, :, 1, :], d[:, :, 1, :], ACT.Exp,
                                             scale=1.0 if r == 0 else -1.0)
                    elif l == 7:
                        ins = act.activation(EE[1], DD[1], ACT.Exp)
                    else:
                        ins = act.activation(EE[0], BF[r], ACT.Exp)
                    ins.then_inc(hg_exp, 1)
                    if l == 2 and before is not None:
                        head_outputs(before)
                    if l == 4 and before is not None:
                        output_roots(before)
                if following is not None:
                    log_gates(*following)
                hold(act, "act", hg_kT_full, unit + 1)
                act.activation(KDT, KV_BANK[:, :], ACT.Copy).then_inc(hg_kT_copied, 1)
                act.activation(EB[:, :], BF[r].rearrange("p (c t) -> p c t", c=NB)[:, :, P - 1 if r == 0 else 0],
                               ACT.Exp).then_inc(hg_decay, 1)
                if before is not None:
                    outputs_transposed(before)

            log_gates(0, 0)
            direction(0, 0, (0, 1))
            with act.Fori(0, HG_HEADS - 1) as i:
                direction(i, 1, (i + 1, 0))
                direction(i + 1, 0, (i + 1, 1), i)
            direction(HG_HEADS - 1, 1, None)
            head_outputs(HG_HEADS - 1)
            output_roots(HG_HEADS - 1)
            outputs_transposed(HG_HEADS - 1)
            for j in range(2):
                for b in range(NB):
                    for n in range(2):
                        drain(POS["up"] + 8 * j + 2 * b + n,
                              copy_to(tm(MKF if j == 0 else H, 0, D, b, n * T, T)))
            act.wait_ge(up_gated, 1)
            for r in range(1):
                act.dma_start(ROW[:, r, :], rows[4].partition_broadcast(P)).then_inc(loaded_rows, 16)
            scaled_transposes("mT", None)
            act.dma_start(MKF[:, 0:2048], subkeys).then_inc(loaded_sub, 16)
            for j in range(2):
                for b in range(NB):
                    drain(POS["out_c"] + 4 * j + b, copy_to(tm(H, 0, D, b, j * T, T)))
                    if j == 1:
                        block_root(b, 16 + b)
            scaled_transposes("xT_f", None)
            with act.Fori(0, 2) as i:
                for j in range(2):
                    pos = POS["wq"] + 8 * j
                    for m in range(4):
                        drain(pos + m, copy_to(QP[:, m, :]), i, 16)
                    for b in range(NB):
                        drain(pos + 4 + b, lambda bk: act.activation(
                            Y[:, ds(i * (2 * T) + (b * 2048 + j * T), T)], bk[:, :], ACT.Copy), i, 16)
                    hold(act, "act", bank_free, i * 16 + (pos + 8 + 4))
                    act.sem_inc(sk_ready, 1)
            act.sem_inc(sk_ready, GROUPS // 2)
            act.sem_inc(acc_free, 1)
            with act.Fori(0, NB) as b:
                with act.Fori(0, PEER_HEADS // 2) as j:
                    for s in range(2):
                        g = b * PEER_HEADS + j * 2 + s
                        hold(act, "act", tanh_in, g + 1)
                        act.activation(EXPS, GW[:, ds(g * 16, 16)], ACT.Exp, accum_out=SUMS)
                        act.activation(TH, GT, ACT.Tanh, scale=GELU_C).then_inc(tanh_out, 1)
                        hold(act, "act", weights, g + 1)
                        for k in range(PEER_K):
                            hold(act, "act", v_done, g * 16 + k + 14)
                            act.activation(DG[k % RING], ident, ACT.Copy, scale=WV[s][:, k:k + 1]
                                           ).then_inc(diag_full, 1)
                hold(act, "act", acc_full, b + 1)
                act.activation(Y[:, ds(b * D, T)], ps[0][:, :], ACT.Copy)
                act.activation(Y[:, ds(b * D + T, T)], ps[1][:, :], ACT.Copy).then_inc(acc_free, 1)
            def projections(blocks):
                for b in blocks:
                    for n in range(2):
                        drain(POS["proj"] + 2 * b + n, copy_to(tm(G, 8, D, b, n * T, T)))

            projections((0, 1))
            act.wait_ge(var_ready, 20)
            act.activation(ST[:, 4:8], ST[:, 4:8], ACT.Sqrt).then_inc(std_ready, 1)
            projections((2, 3))
            scaled_transposes("xT_p", "ple_g")
            for j in range(2):
                for b in range(NB):
                    drain(POS["ple"] + 4 * j + b, lambda bk: act.activation(tm(G, 0, D, b, j * T, T), bk[:, :],
                                                                            ACT.Sigmoid))

        @block.gpsimd
        def _(pool):
            pool.sem_inc(glu_free, 4)
            pool.sem_inc(hg_ke, 1)
            with pool.Fori(0, 3) as i:
                for j in range(4):
                    hold(pool, "pool", bank_free, i * 8 + POS["u"] + 4 + j + 1 + 4)
                    pool.tensor_tensor(hrow(i * 4 + j, TAPS - 1, T), hrow(i * 4 + j, TAPS - 1, T),
                                       SIG[:, j, :], ALU.mult).then_inc(glu_done, 1)
                    hold(pool, "pool", glu_done, i * 4 + j + 1)
                    pool.sem_inc(glu_free, 1)

            def stage_q(src, i, e):
                pool.tensor_copy(QC[:, e, :], src(i, e)).then_inc(q_full, 1)

            def gate(dst, i, e, n):
                pool.tensor_tensor(dst(i, e), dst(i, e), gt_of(dst, i, e), ALU.mult).then_inc(att_gated, 1)

            def attention(name, times, q_of, y_first):
                unit0 = UNITS[name]
                for e in range(2):
                    pool.tensor_copy(QC[:, e, :], q_of(0, e)).then_inc(q_full, 1)

                def gate_pair(i):
                    for e in range(2):
                        hold(pool, "pool", score_free, (unit0 + i) * 10 + (9, 10)[e] + SC)
                        pool.tensor_tensor(yt(i * 2 + (e + y_first)), yt(i * 2 + (e + y_first)),
                                           gt(i * 2 + (e + y_first)), ALU.mult).then_inc(att_gated, 1)

                with pool.Fori(0, times - 1) as i:
                    for e in range(2):
                        hold(pool, "pool", score_full, (unit0 + i) * 10 + (4, 8)[e])
                        pool.tensor_copy(QC[:, e, :], q_of(i + 1, e)).then_inc(q_full, 1)
                    gate_pair(i)
                gate_pair(times - 1)

            pool.wait_ge(bank_free, POS["qm_a"] + 4 + 4)
            attention("mem_a", 2, lambda i, e: yt(i * 2 + (e + 12)), 12)
            for c in range(POOL_GATED):
                pool.wait_ge(silued, c + 1)
                pool.tensor_tensor(yt(c), yt(c), gt(c), ALU.mult).then_inc(mix_gated, 1)
            pool.wait_ge(bank_free, POS["gate_b"] + 16 + 4)
            attention("mem_b", 2, lambda i, e: yt(i * 2 + (e + 12)), 12)
            pool.wait_ge(score_full, UNITS["mem_b"] * 10 + 20)
            attention("dsa", 6, lambda i, e: ht(i * 2 + e), 0)
            pool.wait_ge(rope_done, NB)
            for g in range(2):
                rot = H[:, 6 * T:6 * T + NB * 640].rearrange("p (b c) -> p b c", b=NB)
                for half in range(2):
                    ins = pool.tensor_copy(KK[:, :, g * P + half * 64:g * P + (half + 1) * 64],
                                           rot[:, :, T + g * 64:T + (g + 1) * 64])
                ins.then_inc(kk_ready, 1)
            pool.wait_ge(kk_ready, 2)
            pool.memset(QC[64:P, 0, :], 0.0).then_inc(q_cleared, 1)
            pool.wait_ge(q_cleared, 1)
            pool.memset(QC[0:64, 1, :], 0.0).then_inc(q_cleared, 1)
            pool.wait_ge(q_cleared, 2)
            pool.wait_ge(bank_free, POS["qT"] + 4 + 4)
            for e in range(2):
                pool.tensor_copy(QC[64 * e:64 * e + 64, e, :], Y[64 * e:64 * e + 64, 0:T]).then_inc(q_full, 1)
                pool.wait_ge(q_full, UNITS["gqa"] * 2 + e + 1)
            with pool.Fori(0, 3) as i:
                for e in range(2):
                    hold(pool, "pool", score_full, (UNITS["gqa"] + i) * 10 + (4, 8)[e])
                    pool.tensor_copy(QC[64 * e:64 * e + 64, e, :], Y[64 * e:64 * e + 64, ds(i * T + T, T)]
                                     ).then_inc(q_full, 1)
                    hold(pool, "pool", q_full, (UNITS["gqa"] + i) * 2 + 3 + e)
            with pool.Fori(0, HG_HEADS) as i:
                for r in range(2):
                    unit = i * 2 + r
                    for l in range(LEVELS):
                        hold(pool, "pool", hg_a_full, unit * 8 + max(l - 1, 0) + 1)
                        hold(pool, "pool", hg_exp, unit * 9 + l + 1)
                        pool.tensor_tensor(KE[l % 2], KF[r], EE[l % 2], ALU.mult).then_inc(hg_ke, 1)
                    hold(pool, "pool", hg_exp, unit * 9 + 9)
                    pool.tensor_tensor(QB[r], HQ[:, :, :].rearrange("p h t -> p (h t)")[:, ds(i * T, T)], EE[0],
                                       ALU.mult).then_inc(hg_qb, 1)
            for b in range(NB):
                pool.wait_ge(bank_free, POS["up"] + 2 * b + 2 + 4)
                ins = pool.tensor_tensor(tm(MKF, 0, D, b), tm(MKF, 0, D, b), G[:, b * 2048:b * 2048 + D], ALU.mult)
                ins.then_inc(merged, 1)
            def gather(table, buf, index, loaded, k):
                pool.indirect_dma_start(buf[k % RING], None, table,
                                        bass.IndirectOffsetOnAxis(ap=index[:, k:k + 1], axis=0)
                                        ).then_inc(loaded[k % RING], 16)

            pool.wait_ge(picked, 1)
            pool.tensor_copy(UI[0], IDX[:, 0:16]).then_inc(staged, 1)
            pool.wait_ge(staged, 1)
            for k in range(PEER_K):
                pool.wait_ge(dots, k + 13)
                gather(peer_u, UB, UI[0], u_loaded, k)

            def pair(g, s, last):
                if not last:
                    hold(pool, "pool", picked, g + 2)
                    hold(pool, "pool", dots, g * 16 + 16)
                    pool.tensor_copy(UI[(s + 1) % 2], IDX[:, ds(g * 16 + 16, 16)]).then_inc(staged, 1)
                hold(pool, "pool", v_done, g * 16 + 1)
                pool.tensor_copy(VI[s], IDX[:, ds(g * 16, 16)]).then_inc(staged, 1)
                hold(pool, "pool", staged, g * 2 + (2 if last else 3))
                for k in range(PEER_K):
                    if not last:
                        hold(pool, "pool", dots, g * 16 + 16 + k + 13)
                        gather(peer_u, UB, UI[(s + 1) % 2], u_loaded, k)
                    hold(pool, "pool", v_done, g * 16 + k + 14)
                    gather(peer_v, VB, VI[s], v_loaded, k)

            with pool.Fori(0, GROUPS // 2 - 1) as i:
                for s in range(2):
                    pair(i * 2 + s, s, False)
            pair(GROUPS - 2, 0, False)
            pair(GROUPS - 1, 1, True)

        @block.vector
        def _(dve):
            ch = Chain(dve, "dve", dve_link)
            dve.sem_inc(o_free, 2)
            dve.sem_inc(relu_free, 4)
            dve.sem_inc(hg_exp_used, 1)
            dve.sem_inc(hg_state, 1)

            def row_norm(src, blocks, dst, g, b, done, eps, n):
                for k in range(blocks):
                    for h in range(2):
                        ch.link(dve.bn_stats(ST[:, 8 + 12 * k + 6 * h:14 + 12 * k + 6 * h],
                                             src(k)[:, h * 512:(h + 1) * 512]))
                    ch.link(dve.bn_aggr(MX2[:, 2 * k:2 * k + 2], ST[:, 8 + 12 * k:20 + 12 * k]))
                mv = MX2[:, 0:2 * blocks].rearrange("p (k two) -> p k two", two=2)
                dve.tensor_scalar(ST[:, 4:4 + blocks], mv[:, :, 1], eps, None, ALU.add).then_inc(var_ready, 1)
                dve.wait_ge(std_ready, n)
                ch.link(dve.reciprocal(ST[:, 0:blocks], ST[:, 4:4 + blocks]))
                for k in range(blocks):
                    last = dve.tensor_scalar(dst(k), src(k), mv[:, k, 0:1], ST[:, k:k + 1],
                                             ALU.subtract, ALU.mult)
                    if g is not None:
                        ch.link(last)
                        ch.link(dve.tensor_tensor(dst(k), dst(k), g, ALU.mult))
                        last = dve.tensor_tensor(dst(k), dst(k), b, ALU.add)
                    if k == blocks - 1 or g is not None:
                        last.then_inc(done, 1)
                    else:
                        ch.link(last)

            def attention(name, times, biased, n_keys, scale, dv, joined=False):
                unit0 = UNITS[name]
                per = 8 * ((2 if biased else 1) + 1)

                def body(i):
                    def bias_of(t):
                        b, n = t % 4, n_keys(t % 4)
                        bias = C[:, CC["adm"]:CC["adm"] + P] if b == 0 else MB[:, b - 1, 0:n]
                        d0 = CC["dist"] + 384 - b * P
                        return ch.count(dve.scalar_tensor_tensor(
                            TMP[:, 0:n], C[:, d0:d0 + n], C[:, ds(i * 2 + (CC["slope"] + t // 4), 1)],
                            bias, ALU.mult, ALU.add))

                    bias_made = bias_of(0) if biased else None
                    for t in range(10):
                        if t < 8:
                            b = t % 4
                            n = n_keys(b)
                            mx, nm = MX[:, b:b + 1], NM[:, b:b + 1]
                            s = SC_BANK[t % SC]
                            if biased:
                                ch.after(bias_made)
                            hold(dve, "dve", score_full, (unit0 + i) * 10 + t + 1)
                            if biased:
                                ch.link(dve.tensor_tensor_reduce(
                                    out=L[:, b, 0:n], in0=s[:, 0:n], in1=TMP[:, 0:n], scale=scale,
                                    scalar=-3e38, op0=ALU.add, op1=ALU.max, accum_out=mx))
                            else:
                                ch.link(dve.tensor_reduce(mx, s[:, 0:n], AX.X, ALU.max))
                            dve.tensor_scalar(nm, mx, -1.0 if biased else -scale, None, ALU.mult
                                              ).then_inc(maxed, 1)
                            if biased and t < 7:
                                bias_made = bias_of(t + 1)
                        if t >= 2:
                            u = t - 2
                            e, b = u // 4, u % 4
                            hold(dve, "dve", pv_full, (unit0 + i) * 8 + u + 1)
                            ch.link(dve.reciprocal(RI[:, b:b + 1], SM[:, b:b + 1]))
                            if joined:
                                if u in (0, 2):
                                    hold(dve, "dve", os_free, (unit0 + i) * 2 + u // 2 + 1)
                                dst = OS[:, b // 2, (b % 2) * P + e * dv:(b % 2) * P + (e + 1) * dv]
                            else:
                                if b == 0:
                                    hold(dve, "dve", os_free, (unit0 + i) * 2 + e + 1)
                                dst = OS[:, e, b * P:(b + 1) * P]
                            dve.tensor_scalar(dst, O_BANK[u % 2][:, 0:dv], RI[:, b:b + 1], None,
                                              ALU.mult).then_inc(o_free, 1)

                ch.loop(times, per, body)

            dve.memset(ONES[:, :], 1.0).then_inc(ones_ready, 1)
            dve.wait_ge(loaded_mem, 16)
            row_norm(lambda k: mem_tm[:, k * D:(k + 1) * D], 2, lambda k: mem_tm[:, k * D:(k + 1) * D],
                     None, None, mem_normed, LN_EPS, 1)
            hp = H[:, 0:CONV_T * HROW].rearrange("p (c t) -> p c t", c=CONV_T)
            ch.link(dve.memset(hp[:, :, 0:TAPS - 1], 0.0))
            dve.wait_ge(loaded_const, 48)
            with dve.Fori(0, CONV_T // 2) as i:
                for k in range(TAPS):
                    for j in range(2):
                        c = i * 2 + j
                        if k == 0:
                            hold(dve, "dve", glu_done, c + 1)
                            ins = dve.tensor_scalar(yt(c), hrow(c, k, T), V[:, ds(c * TAPS + FM["conv_w"], 1)],
                                                    V[:, ds(c + FM["conv_b"], 1)], ALU.mult, ALU.add)
                        else:
                            dve.wait_ge(conv_tap, i * (2 * TAPS) + (2 * k + j - 1))
                            ins = dve.scalar_tensor_tensor(yt(c), hrow(c, k, T),
                                                           V[:, ds(c * TAPS + (FM["conv_w"] + k), 1)],
                                                           yt(c), ALU.mult, ALU.add)
                        ins.then_inc(conv_tap, 1)
            attention("mem_a", 2, False, lambda b: N_MEM, SCALE128, P)
            dve.wait_ge(bank_free, POS["ln"] + 1 + 4)
            for c in range(CONV_T):
                dve.tensor_tensor(yt(c), yt(c), MU[:, 0, :], ALU.subtract).then_inc(centred, 1)
            dve.wait_ge(bank_free, POS["ln"] + 2 + 4)
            dve.tensor_scalar(MU[:, 1, :], MU[:, 1, :], LN_EPS, None, ALU.add).then_inc(var_ready, 1)
            dve.wait_ge(std_ready, 2)
            ch.link(dve.reciprocal(MU[:, 0, :], MU[:, 1, :]))
            for c in range(CONV_T):
                dve.tensor_tensor(yt(c), yt(c), MU[:, 0, :], ALU.mult).then_inc(scaled, 1)
            for c in range(POOL_GATED, CONV_T):
                dve.wait_ge(silued, c + 1)
                dve.tensor_tensor(yt(c), yt(c), gt(c), ALU.mult).then_inc(mix_gated, 1)

            def layer_end(name, n, rows_at, rest=None):

                def residual(half, b):
                    cols = slice(half * T, (half + 1) * T)
                    dve.wait_ge(bank_free, POS[name] + 4 * half + b + 1 + 4)
                    ch.link(dve.scalar_tensor_tensor(X[:, b, cols], X[:, b, cols], ALPHA,
                                                     RES[:, b * D + half * T:b * D + (half + 1) * T],
                                                     ALU.mult, ALU.add))
                    at = 8 + 12 * b + 6 * half
                    ch.link(dve.bn_stats(ST[:, at:at + 6], X[:, b, cols]))

                for b in range(NB):
                    residual(0, b)
                dve.wait_ge(loaded_rows, 32 * rows_at)
                for b in range(NB):
                    residual(1, b)
                    ch.link(dve.bn_aggr(MX2[:, 2 * b:2 * b + 2], ST[:, 8 + 12 * b:20 + 12 * b]))
                    dve.tensor_scalar(ST[:, 4 + b:5 + b], MX2[:, 2 * b + 1:2 * b + 2], LN_EPS, None, ALU.add
                                      ).then_inc(var_ready, 1)
                    n += 1
                    dve.wait_ge(std_ready, n)
                    ch.link(dve.reciprocal(ST[:, b:b + 1], ST[:, 4 + b:5 + b]))
                    ch.link(dve.tensor_scalar(X[:, b, :], X[:, b, :], MX2[:, 2 * b:2 * b + 1], ST[:, b:b + 1],
                                              ALU.subtract, ALU.mult))
                    ch.link(dve.tensor_tensor(X[:, b, :], X[:, b, :], ROW[:, 0, :], ALU.mult))
                    dve.tensor_tensor(X[:, b, :], X[:, b, :], ROW[:, 1, :], ALU.add).then_inc(x_normed, 1)
                    if rest is not None:
                        n += 1
                        rest(b, n)

            dve.wait_ge(loaded_x, 32)
            layer_end("out_a", 2, 1)
            dve.wait_ge(x_normed, NB)
            for b in range(1, NB):
                n = (b + 1) * P
                for h in range(IDX_HEADS):
                    dve.wait_ge(bank_free, POS["index"] + (b - 1) * IDX_HEADS + h + 1 + 4)
                    w = WI[:, b, h:h + 1]
                    if h == 0:
                        ins = dve.tensor_scalar(MB[:, b - 1, 0:n], SIG[:, h % 4, 0:n], w, None, ALU.mult)
                    else:
                        ins = dve.scalar_tensor_tensor(MB[:, b - 1, 0:n], SIG[:, h % 4, 0:n], w,
                                                       MB[:, b - 1, 0:n], ALU.mult, ALU.add)
                    ins.then_inc(relu_free, 1)
                    dve.wait_ge(relu_free, 4 + (b - 1) * IDX_HEADS + h + 1)
                adm = C[:, CC["adm"]:CC["adm"] + P]
                ch.link(dve.tensor_tensor(MB[:, b - 1, n - P:n], MB[:, b - 1, n - P:n], adm, ALU.add))

            index = [MB[:, b - 1, 0:(b + 1) * P] for b in range(1, NB)]

            def take(i):
                found = [ch.count(dve.max(TOP8[:, b, :], index[b])) for b in range(NB - 1)]
                for b in range(NB - 1):
                    ch.after(found[b])
                    last = ch.count(dve.match_replace(index[b], TOP8[:, b, :], index[b], TAKEN))
                ch.after(last)

            ch.loop(TOPK // 8, 2 * (NB - 1), take)
            for b in range(1, NB):
                own = index[b - 1][:, b * P:(b + 1) * P]
                ch.link(dve.tensor_scalar(index[b - 1], index[b - 1], -2e38, NEG, ALU.is_ge, ALU.mult))
                ch.link(dve.tensor_tensor(own, own, adm, ALU.add))
            attention("mem_b", 2, False, lambda b: N_MEM, SCALE128, P)
            attention("dsa", 6, True, lambda b: (b + 1) * P, SCALE128, P)

            def rms_sum(b, col):
                ch.link(dve.tensor_tensor_reduce(out=RES[:, b * D:(b + 1) * D], in0=X[:, b, :], in1=X[:, b, :],
                                                 scale=1.0, scalar=0.0, op0=ALU.mult, op1=ALU.add,
                                                 accum_out=ST[:, col + b:col + b + 1]))

            def rms_block(b, n):
                rms_sum(b, 56)
                dve.tensor_scalar(ST[:, 4 + b:5 + b], ST[:, 56 + b:57 + b], 1.0 / D, RMS_EPS, ALU.mult, ALU.add
                                  ).then_inc(var_ready, 1)
                dve.wait_ge(std_ready, n)
                ch.link(dve.reciprocal(ST[:, b:b + 1], ST[:, 4 + b:5 + b]))
                return dve.tensor_scalar(RES[:, b * D:(b + 1) * D], X[:, b, :], ST[:, b:b + 1], None, ALU.mult)

            def mixer_rows(b, n):
                dve.wait_ge(x_normed, NB + b + 1)
                rms_block(b, n).then_inc(xn_ready, 1)

            layer_end("out_b", 6, 2, mixer_rows)
            dve.tensor_tensor(LB[:, :], fm("lb0", 0, 8), fm("lb1", 0, 8), ALU.subtract).then_inc(lb_diff, 1)
            dve.wait_ge(lb_sig, 1)
            ch.link(dve.tensor_scalar(OML[:, :], LB[:, :], -1.0, 1.0, ALU.mult, ALU.add))
            dve.wait_ge(bank_free, POS["akv"] + 4 + 4)
            rot = H[:, 6 * T:6 * T + NB * 640].rearrange("p (b c) -> p b c", b=NB)
            for b in range(NB):
                src = tm(H, 0, QKV, b, 0, 640)
                ch.link(dve.tensor_tensor(rot[:, b, :], src, src, ALU.mult))
                ch.link(dve.tensor_reduce(RS[:, 10 * b:10 * b + 10], rot[:, b, :].rearrange("p (h d) -> p h d", d=64),
                                          AX.X, ALU.add))
            dve.tensor_scalar(RS[:, :], RS[:, :], 1.0 / 64, RMS_EPS, ALU.mult, ALU.add).then_inc(var_ready, 1)
            dve.wait_ge(std_ready, 15)
            ch.link(dve.reciprocal(RS[:, :], RS[:, :]))
            dve.wait_ge(loaded_qkn, 16)
            for b in range(NB):
                src = tm(H, 0, QKV, b, 0, 640)
                s3 = src.rearrange("p (h d) -> p h d", d=64)
                scale = RS[:, 10 * b:10 * b + 10].rearrange("p (h o) -> p h o", o=1).broadcast_to([P, ROPE_HEADS, 64])
                ch.link(dve.tensor_tensor(s3, s3, scale, ALU.mult))
                ch.link(dve.tensor_tensor(src, src, QKN, ALU.mult))
                s5 = src.rearrange("p (h a x d) -> p h a x d", h=ROPE_HEADS, a=2, x=2)
                r5 = rot[:, b, :].rearrange("p (h a x d) -> p h a x d", h=ROPE_HEADS, a=2, x=2)
                cos, sin = ([C[:, CC[t] + 32 * b:CC[t] + 32 * b + 32].rearrange("p (o a d) -> p o a d", o=1, a=2)
                             .broadcast_to([P, ROPE_HEADS, 2, 16]) for t in ("cos", "sin")])
                t4 = TMPR[:, 0:320].rearrange("p (h a d) -> p h a d", h=ROPE_HEADS, a=2)
                x1, x2, y1, y2 = s5[:, :, :, 0, :], s5[:, :, :, 1, :], r5[:, :, :, 0, :], r5[:, :, :, 1, :]
                ch.link(dve.tensor_tensor(y1, x1, cos, ALU.mult))
                ch.link(dve.tensor_tensor(t4, x2, sin, ALU.mult))
                ch.link(dve.tensor_tensor(y1, y1, t4, ALU.subtract))
                ch.link(dve.tensor_tensor(y2, x1, sin, ALU.mult))
                ch.link(dve.tensor_tensor(t4, x2, cos, ALU.mult))
                dve.tensor_tensor(y2, y2, t4, ALU.add).then_inc(rope_done, 1)
                dve.wait_ge(rope_done, b + 1)
            dve.wait_ge(bank_free, POS["hfb"] + 4 + 4)
            for m in range(2 * HG_HEADS):
                gates = MKF[:, m * T:(m + 1) * T]
                ins = dve.tensor_scalar(gates, gates, OML[:, m:m + 1], LB[:, m:m + 1], ALU.mult, ALU.add)
                if m == 2 * HG_HEADS - 1:
                    ch.link(ins)
            attention("gqa", 4, False, lambda b: T, 0.125, 64, joined=True)
            dve.wait_ge(score_free, UNITS["end"] * 10 + SC)
            dve.wait_ge(loaded_levels, 16)
            dve.sem_inc(hg_a_free, 2)
            for r in range(2):
                ch.link(dve.memset(AS[r], 0.0))
            hq = HQ[:, :, :].rearrange("p h t -> p (h t)")

            def keys(i, r):
                dve.tensor_scalar(KF[r], MKF[:, ds(i * T + r * (4 * T), T)], -1.0, 1.0, ALU.mult, ALU.add
                                  ).then_inc(hg_f, 1)

            def running_sums(i, r):
                hold(dve, "dve", hg_lf, i * 2 + r + 1)
                for c in range(NB):
                    seg, out = LF[:, c * P:(c + 1) * P], BF[r][:, c * P:(c + 1) * P]
                    if r == 1:
                        seg, out = seg[:, ::-1], out[:, ::-1]
                    ins = dve.tensor_tensor_scan(out, ONES[:, :], seg, 0.0, ALU.mult, ALU.add)
                ch.link(ins)

            def mean_squares(i):
                hold(dve, "dve", hg_o_copied, i + 1)
                dve.tensor_scalar(RS[:, 0:4], ST[:, 8:12], 1.0 / P, RMS_EPS, ALU.mult, ALU.add).then_inc(hg_ms, 1)

            def output_scales(i):
                hold(dve, "dve", hg_std, i + 1)
                ch.link(dve.reciprocal(ST[:, 0:4], RS[:, 0:4]))

            def normed_output(i, c):
                o = OH[:, c * P:(c + 1) * P]
                ch.link(dve.scalar_tensor_tensor(o, o, ST[:, c:c + 1], HROWN[:, :], ALU.mult, ALU.mult))
                dve.tensor_tensor(o, o, tm(Y, 12, T, c, i * P, P), ALU.mult).then_inc(hg_normed, 1)

            def direction(i, r, following, before=None):
                unit = i * 2 + r
                base = BF[r]

                def add_level(l):
                    if l == 0 and before is not None:
                        hold(dve, "dve", hg_o_full, before + 1)
                    hold(dve, "dve", hg_a_free, unit * 8 + l + 2)
                    hold(dve, "dve", hg_a_full, unit * 8 + l + 2)
                    mask = (LVL[:, r, l, :] if l < LEVELS else ident).rearrange("p (o t) -> p o t", o=1)
                    dve.copy_predicated(AS[r].rearrange("p (c t) -> p c t", c=NB),
                                        mask.bitcast(U32).broadcast_to([P, NB, P]),
                                        A_BANK[l % 2][:, :].rearrange("p (c t) -> p c t", c=NB)
                                        ).then_inc(hg_a_free, 1)

                for t in range(10):
                    if t < 8:
                        if t < LEVELS:
                            m = 64 >> t
                            b3 = base.rearrange("p (b m) -> p b m", m=2 * m)
                            d3 = DD[t % 2].rearrange("p (b m) -> p b m", m=2 * m)
                            at = m - 1 if r == 0 else m
                            ref = b3[:, :, at:at + 1].broadcast_to([P, T // (2 * m), 2 * m])
                            ins = dve.tensor_tensor(d3, b3, ref, ALU.subtract)
                        else:
                            b3 = base.rearrange("p (c t) -> p c t", c=NB)
                            d3 = DD[1].rearrange("p (c t) -> p c t", c=NB)
                            at = P - 1 if r == 0 else 0
                            ref = b3[:, :, at:at + 1].broadcast_to([P, NB, P])
                            ins = dve.tensor_tensor(d3, ref, b3, ALU.subtract)
                        ins.then_inc(hg_diff, 1)
                    if t == 0 and following is not None:
                        keys(*following)
                    if 1 <= t:
                        l = t - 1
                        hold(dve, "dve", hg_exp, unit * 9 + l + 1)
                        if l < LEVELS:
                            dve.tensor_tensor(QE[l % 2], hq[:, ds(i * T, T)], EE[l % 2], ALU.mult
                                              ).then_inc(hg_qe, 1)
                        elif l == 7:
                            dve.tensor_tensor(KDEC, KF[r], EE[1], ALU.mult).then_inc(hg_kdec, 1)
                        else:
                            pass
                    if 2 <= t:
                        add_level(t - 2)
                    if 1 <= t:
                        l = t - 1
                        if l < LEVELS:
                            hold(dve, "dve", hg_qe, unit * LEVELS + l + 1)
                        else:
                            hold(dve, "dve", hg_kdec if l == 7 else hg_qb, unit + 1)
                        dve.sem_inc(hg_exp_used, 1)
                    if before is not None:
                        if t == 4:
                            mean_squares(before)
                        if t == 6:
                            output_scales(before)
                        if 6 <= t:
                            normed_output(before, t - 6)
                if following is not None:
                    running_sums(*following)
                hold(dve, "dve", hg_kv_full, unit + 1)
                order = [0, 1, 2] if r == 0 else [3, 2, 1]
                step = 1 if r == 0 else -1
                for n, c in enumerate(order):
                    new = STATE[r][:, (c + step) * P:(c + step + 1) * P]
                    kv = KV_BANK[:, c * P:(c + 1) * P]
                    if n == 0:
                        ch.link(dve.tensor_copy(new, kv))
                        hold(dve, "dve", hg_decay, unit + 1)
                    else:
                        ins = dve.scalar_tensor_tensor(new, STATE[r][:, c * P:(c + 1) * P], EB[:, c:c + 1], kv,
                                                       ALU.mult, ALU.add)
                        if n == 1:
                            ch.link(ins)
                        else:
                            ins.then_inc(hg_state, 1)

            def head(i):
                direction(i, 1, (i + 1, 0))
                direction(i + 1, 0, (i + 1, 1), i)

            keys(0, 0)
            running_sums(0, 0)
            direction(0, 0, (0, 1))
            ch.loop(HG_HEADS - 1, 2 * (1 + 2) + 1 + NB, head)
            direction(HG_HEADS - 1, 1, None)
            mean_squares(HG_HEADS - 1)
            output_scales(HG_HEADS - 1)
            for c in range(NB):
                normed_output(HG_HEADS - 1, c)
            for b in range(NB):
                dve.wait_ge(bank_free, POS["up"] + 8 + 2 * b + 2 + 4)
                rec = tm(H, 0, D, b)
                ch.link(dve.tensor_tensor(rec, rec, G[:, b * 2048 + D:(b + 1) * 2048], ALU.mult))
                dve.wait_ge(merged, b + 1)
                ins = dve.tensor_tensor(tm(MKF, 0, D, b), tm(MKF, 0, D, b), rec, ALU.add)
                if b < NB - 1:
                    ch.link(ins)
            ins.then_inc(up_gated, 1)
            for half in range(2):
                for b in range(NB):
                    cols = slice(half * T, (half + 1) * T)
                    dve.wait_ge(bank_free, POS["out_c"] + 4 * half + b + 1 + 4)
                    ch.link(dve.tensor_tensor(X[:, b, cols], X[:, b, cols], tm(H, 0, D, b, half * T, T), ALU.add))
                    if half == 1:
                        ch.link(rms_block(b, 16 + b))
                        dve.wait_ge(loaded_rows, 32 * 2 + 16)
                        dve.tensor_tensor(tm(H, 0, D, b), tm(H, 0, D, b), ROW[:, 0, :], ALU.mult
                                          ).then_inc(h_ready, 1)
            dve.memset(ZERO[:, :], 0.0).then_inc(zero_ready, 1)
            dve.wait_ge(sk_ready, 1)
            dve.wait_ge(h_ready, NB)

            shape = [P, 16, 16]

            def first(a):
                return a.rearrange("p (k o) -> p k o", o=1).broadcast_to(shape)

            def second(a):
                return a.rearrange("p (o k) -> p o k", o=1).broadcast_to(shape)

            def square(a):
                return a.rearrange("p (i j) -> p i j", i=16)

            def top16_step(n, values, val, idx):
                half = slice(0, 8) if n < 3 else slice(8, 16)
                if n in (0, 3):
                    ch.link(dve.max(val[:, half], values))
                elif n in (1, 4):
                    ch.link(dve.max_index(idx[:, half], val[:, half], values))
                else:
                    ch.link(dve.match_replace(values, val[:, half], values, TAKEN))

            def route_step(g, k):
                if k == 0:
                    ch.link(dve.tensor_copy(WS, Y[:, ds(g * 256, 256)]))
                if k < 5:
                    for q in range(2):
                        top16_step(k, WS[:, q * P:(q + 1) * P], TOPV[:, q * 16:q * 16 + 16],
                                   TOPI[:, q * 16:q * 16 + 16])
                if k == 5:
                    ch.link(dve.tensor_copy(TOPF, TOPI))
                    ch.link(dve.tensor_tensor(square(CAND), first(TOPV[:, 0:16]), second(TOPV[:, 16:32]), ALU.add))
                if 6 <= k < 11:
                    top16_step(k - 6, CAND, BEST, BESTI)
                if k == 11:
                    ch.link(dve.tensor_scalar(PARTI[:, 0:16], BESTI, 4, None, ALU.logical_shift_right))
                    ch.link(dve.tensor_scalar(PARTI[:, 16:32], BESTI, 15, None, ALU.bitwise_and))
                    ch.link(dve.tensor_copy(PARTF, PARTI))
                if k in (12, 13):
                    a = k - 12
                    rank = C[:, CC["iota"]:CC["iota"] + 16]
                    ch.link(dve.tensor_tensor(square(HOT), first(PARTF[:, a * 16:a * 16 + 16]), second(rank),
                                              ALU.is_equal))
                    ch.link(dve.tensor_tensor(square(HOT), square(HOT), second(TOPF[:, a * 16:a * 16 + 16]), ALU.mult))
                    ch.link(dve.tensor_reduce(PICK[:, a * 16:a * 16 + 16], square(HOT), AX.X, ALU.add))
                if k == 14:
                    ch.link(dve.scalar_tensor_tensor(PICK[:, 0:16], PICK[:, 0:16], float(P), PICK[:, 16:32],
                                                     ALU.mult, ALU.add))
                if k == 15:
                    dve.tensor_scalar(GW[:, ds(g * 16, 16)], BEST, BEST[:, 0:1], None, ALU.subtract)
                    dve.tensor_copy(IDX[:, ds(g * 16, 16)], PICK[:, 0:16]).then_inc(picked, 1)
                    hold(dve, "dve", picked, g + 1)

            ROUTE_LINKS = 1 + 10 + 2 + 5 + 3 + 6 + 1

            def wait_dve(semaphore, value):
                if isinstance(value, int):
                    dve.wait_ge(semaphore, value)
                else:
                    hold(dve, "dve", semaphore, value)

            def weigh(g, s, ahead):
                for k in range(PEER_K):
                    wait_dve(u_loaded[k % RING], g * 64 + 16 * (k // RING + 1))
                    wait_dve(dots, g * 16 + k + 15)
                    dve.tensor_tensor_reduce(out=JUNK[k % 2], in0=UB[k % RING], in1=HC, scale=1.0, scalar=0.0,
                                             op0=ALU.mult, op1=ALU.add, accum_out=AA[s][:, k:k + 1]
                                             ).then_inc(dots, 1)
                    if ahead:
                        route_step(g + 2, k)
                wait_dve(dots, g * 16 + 32)
                a = AA[s]
                ch.link(dve.tensor_tensor(GT, a, a, ALU.mult))
                ch.link(dve.tensor_scalar(GT, GT, 0.044715, 1.0, ALU.mult, ALU.add))
                dve.tensor_tensor(GT, GT, a, ALU.mult).then_inc(tanh_in, 1)
                wait_dve(tanh_out, g + 1)
                dve.reciprocal(RSUM, SUMS)
                ch.link(dve.scalar_tensor_tensor(TH, TH, 1.0, a, ALU.add, ALU.mult))
                ch.link(dve.tensor_scalar(TH, TH, RSUM, 0.5, ALU.mult, ALU.mult))
                dve.tensor_tensor(WV[s], TH, EXPS, ALU.mult).then_inc(weights, 1)

            WEIGH_LINKS = 4

            def two_groups(i, ahead):
                if ahead:
                    hold(dve, "dve", sk_ready, i + 2)
                ch.link(dve.tensor_copy(HC, H[:, ds((i // (PEER_HEADS // 2)) * D, D)]))
                for s in range(2):
                    weigh(i * 2 + s, s, ahead)

            dve.sem_inc(dots, 16)

            def route(g):
                for k in range(PEER_K):
                    route_step(g, k)

            ch.loop(2, ROUTE_LINKS, route)
            ch.loop(GROUPS // 2 - 1, 1 + 2 * (ROUTE_LINKS + WEIGH_LINKS), lambda i: two_groups(i, True))
            two_groups(GROUPS // 2 - 1, False)
            for b in range(NB):
                dve.wait_ge(acc_free, b + 2)
                ch.link(dve.tensor_tensor(X[:, b, :], X[:, b, :], tm(Y, 0, D, b), ALU.add))
                rms_sum(b, 8)
            dve.tensor_scalar(ST[:, 4:8], ST[:, 8:12], 1.0 / D, RMS_EPS, ALU.mult, ALU.add).then_inc(var_ready, 1)
            dve.wait_ge(std_ready, 20)
            ch.link(dve.reciprocal(ST[:, 0:4], ST[:, 4:8]))
            for b in range(NB):
                ins = dve.tensor_scalar(RES[:, b * D:(b + 1) * D], X[:, b, :], ST[:, b:b + 1], None, ALU.mult)
                if b < NB - 1:
                    ch.link(ins)
            ins.then_inc(xn_ready, 1)
            for b in range(NB):
                dve.wait_ge(bank_free, POS["ple"] + 4 + b + 1 + 4)
                ch.link(dve.tensor_tensor(tm(G, 0, D, b), tm(G, 0, D, b), tm(G, 8, D, b), ALU.mult))
                dve.tensor_tensor(X[:, b, :], X[:, b, :], tm(G, 0, D, b), ALU.add).then_inc(y_ready, 1)


def shape_constants():
    q, m = np.arange(P)[:, None], np.arange(896)[None, :]
    dist = np.abs(q - (m - 384))
    adm = np.where(np.arange(P)[None, :] // CHUNK <= q // CHUNK, 0.0, NEG)
    base = [2.0 ** (-8.0 * (i + 1) / 8) for i in range(8)]
    extra = [2.0 ** (-4.0 * (2 * i + 1) / 8) for i in range(HEADS_B - 8)]
    slope = np.broadcast_to(-np.float32(base + extra) / np.float32(SCALE128), (P, HEADS_B))
    t = np.arange(T)
    inv = (10000.0 ** (-np.arange(16, dtype=np.float32) / 16)).astype(np.float32)
    ang = np.stack([(t // 64).astype(np.float32)[:, None] * inv, (t % 64).astype(np.float32)[:, None] * inv], 1)
    table = lambda v: v.reshape(NB, P, 32).transpose(1, 0, 2).reshape(P, -1)
    return np.concatenate([np.eye(P), dist, adm, slope, table(np.cos(ang)), table(np.sin(ang)),
                           np.broadcast_to(np.arange(16), (P, 16))],
                          1).astype(np.float32)


def level_masks():
    s, t = np.arange(P)[:, None], np.arange(P)[None, :]
    fwd = [(s // (2 * m) == t // (2 * m)) & (s % (2 * m) < m) & (t % (2 * m) >= m)
           for m in (64 >> l for l in range(LEVELS))]
    bwd = [a.T for a in fwd]
    return np.concatenate(fwd + bwd, 1).astype(np.float32)


def slots_of(w, n=T):
    s = [w[:, c:c + n].reshape(KD, P, n).transpose(1, 0, 2) for c in range(0, w.shape[1], n)]
    return [a.reshape(P, -1) for a in s]


def out_slots(w):
    return [w[k:k + D, n:n + T].reshape(KD, P, T).transpose(1, 0, 2).reshape(P, -1)
            for n in range(0, w.shape[1], T) for k in range(0, w.shape[0], D)]


def lay_out(i):
    f = lambda v: v.reshape(-1, P).T
    aw, bw = i["a_w_in"][0], i["b_w_in"][0]
    a, gl = slots_of(aw[:, 0:1536]), slots_of(aw[:, 1536:3072])
    w = slots_of(i["a_w_mkv"][0]) + slots_of(i["b_w_mkv"][0])
    w += [s for pair in zip(a, gl) for s in pair]
    w += slots_of(aw[:, 3584:5632]) + slots_of(aw[:, 3072:3584]) + out_slots(i["a_w_out"][0])
    spec = np.concatenate([bw[:, 2048:2304], bw[:, 2304:2368], bw[:, 2304:2368], bw[:, 2368:2376],
                           np.zeros((D, 120), bw.dtype)], 1)
    w += slots_of(bw[:, 0:2048]) + slots_of(spec) + slots_of(bw[:, 2376:2888]) + slots_of(bw[:, 2888:4936])
    w += out_slots(i["b_w_out"][0])
    cw = i["w_in_2"][0]
    akv = np.concatenate([cw[:, 512:768], np.zeros((D, 256), cw.dtype)], 1)
    w += slots_of(cw[:, 0:512]) + slots_of(akv) + slots_of(cw[:, 768:])
    w += [i[n][0].reshape(4, P, D).transpose(1, 0, 2).reshape(P, -1) for n in ("w_up_att_2", "w_up_hg_2")]
    w += slots_of(i["w_out_2"][0]) + slots_of(i["peer_wq_2"][0])
    proj = i["ple_proj_2"][0].reshape(2, P, D).transpose(1, 0, 2).reshape(P, -1)
    w += [np.concatenate([proj, np.zeros_like(proj)], 1)] + slots_of(i["ple_gate_2"][0])
    sub = i["peer_subkeys_2"][0].reshape(16, P, P).transpose(2, 0, 1).reshape(P, -1)
    norm_rows = np.concatenate([np.tile(i["q_norm_2"][0], 8), np.tile(i["k_norm_2"][0], 2), i["hg_out_norm_2"][0]])
    conv = i["a_conv_w"][0].T.reshape(CONV_T, P, TAPS).transpose(1, 0, 2).reshape(P, -1)
    fmvec = np.concatenate([f(i["mem_ln_g"]), f(i["mem_ln_b"]), f(i["a_conv_b"][0]), f(i["a_ln_g"][0]),
                            f(i["a_ln_b"][0]), conv, f(i["norm_mix_2"][0]), f(i["norm_ple_2"][0]),
                            f(i["hg_lb_raw_2"][0]), f(i["hg_lb_raw_2"][1])], 1)
    rows = np.stack([i["a_post_g"][0], i["a_post_b"][0], i["b_post_g"][0], i["b_post_b"][0],
                     i["norm_ffn_2"][0]])
    return {"x": i["x"][0], "xT": i["x"][0].T, "mem": i["mem"][0], "wstream": np.stack(w), "fmvec": fmvec,
            "rows": rows, "norm_rows": norm_rows, "consts": shape_constants(), "levels": level_masks(),
            "subkeys": sub, "pT": i["p_2"][0, 0].T, "peer_u": i["peer_u_2"][0], "peer_v": i["peer_v_2"][0]}


OUT_SHAPE = (1, T, D)


def kernel(**inputs):
    import concourse.bacc as bacc
    from concourse.bass_utils import run_bass_kernel_spmd as run

    arrays = {k: np.ascontiguousarray(v) for k, v in lay_out({k: np.asarray(v) for k, v in inputs.items()}).items()}
    nc = bacc.Bacc("TRN2", target_bir_lowering=False, num_devices=1)
    args = {k: nc.dram_tensor(k, v.shape, mybir.dt.from_np(v.dtype), kind="ExternalInput").ap()
            for k, v in arrays.items()}
    args["out"] = nc.dram_tensor("out", OUT_SHAPE, F32, kind="ExternalOutput").ap()
    program(nc, **args)
    return run(nc, [arrays], core_ids=[0]).results[0]["out"]
```
